# Optimizing a Trainium2 kernel written in Bass

```python
import math
import jax, jax.numpy as jnp
from jax import lax
import numpy as np

D_MODEL = 1024
BATCH = 1
SEQ = 512
DEPTH = 2

D_MIX = D_MODEL
S5_WIDTH = D_MIX // 4
S5_GROUP = 16
S5_GROUPS = S5_WIDTH // S5_GROUP
S5_STATE = 64
CONV_WIDTH = D_MIX // 4
CONV_K = 3
HG_WIDTH = D_MIX // 2
HG_HEAD_DIM = 128
HG_HEADS = HG_WIDTH // HG_HEAD_DIM
HG_CHUNK = 64
IN_SPLITS = (S5_WIDTH, CONV_WIDTH, CONV_WIDTH, CONV_WIDTH, HG_WIDTH, HG_WIDTH, HG_WIDTH, HG_WIDTH)
D_IN = S5_WIDTH + 3 * CONV_WIDTH + 4 * HG_WIDTH
D_FF = (7 * D_MODEL) // 2
N_EXPERTS = 8
TOP_K = 2
MOE_BLOCK = 128
N_DENSE = (DEPTH + 1) // 2
N_MOE = DEPTH // 2
NORM_EPS = 1e-6
DT_MIN = 1e-3
DT_MAX = 1e-1
LB_FLOOR = 1e-30

kernel_name = "hybrid_s5_conv_hgrn2_moe"

F32 = jnp.float32

def rmsnorm(x, g):
    x32 = x.astype(F32)
    y = x32 * lax.rsqrt(jnp.mean(x32 * x32, axis=-1, keepdims=True) + NORM_EPS)
    return (y * g.astype(F32)).astype(x.dtype)

def split_cols(h):
    parts, off = [], 0
    for w in IN_SPLITS:
        parts.append(h[..., off:off + w])
        off += w
    return parts

def _diag_scan_op(e1, e2):
    a1, b1 = e1
    a2, b2 = e2
    return a1 * a2, a2 * b1 + b2

def s5_mixer(u, lam_re, lam_im, log_dt, b_re, b_im, c_re, c_im, d, w_glu):
    bsz, L, _ = u.shape
    ug = u.astype(F32).reshape(bsz, L, S5_GROUPS, S5_GROUP)
    lam = lax.complex(lam_re.astype(F32), lam_im.astype(F32))
    dt = jnp.exp(log_dt.astype(F32))[:, None]
    lam_bar = jnp.exp(lam * dt)
    b = lax.complex(b_re.astype(F32), b_im.astype(F32))
    b_bar = ((lam_bar - 1.0) / lam)[..., None] * b
    bu = jnp.einsum('gpc,blgc->blgp', b_bar, ug.astype(jnp.complex64))
    a = jnp.broadcast_to(lam_bar, bu.shape)
    _, states = lax.associative_scan(_diag_scan_op, (a, bu), axis=1)
    c = lax.complex(c_re.astype(F32), c_im.astype(F32))
    y = jnp.real(jnp.einsum('gcp,blgp->blgc', c, states)) + d.astype(F32).reshape(S5_GROUPS, S5_GROUP) * ug
    y = jax.nn.gelu(y.reshape(bsz, L, S5_WIDTH))
    return y * jax.nn.sigmoid(y @ w_glu.astype(F32))

def conv_mixer(gate_b, gate_c, v, conv_w):
    z = gate_c * v
    L = z.shape[1]
    zp = jnp.pad(z, ((0, 0), (CONV_K - 1, 0), (0, 0)))
    y = zp[:, 0:L] * conv_w[0]
    for k in range(1, CONV_K):
        y = y + zp[:, k:k + L] * conv_w[k]
    return gate_b * y

def hgrn2_mixer(q, f_pre, i_val, gate, lb, norm_g):
    bsz, L, _ = q.shape
    n_chunks = L // HG_CHUNK

    def heads(t):
        return t.astype(F32).reshape(bsz, n_chunks, HG_CHUNK, HG_HEADS, HG_HEAD_DIM).transpose(1, 0, 3, 2, 4)

    lbh = jnp.clip(lb.astype(F32), 0.0, 1.0 - 1e-6).reshape(HG_HEADS, 1, HG_HEAD_DIM)
    fp = heads(f_pre)
    log_f = jnp.logaddexp(jnp.log(jnp.maximum(lbh, LB_FLOOR)), jnp.log1p(-lbh) + jax.nn.log_sigmoid(fp))
    k = (1.0 - lbh) * jax.nn.sigmoid(-fp)
    qh = jax.nn.silu(heads(q))
    vh = heads(i_val)
    mask = jnp.tril(jnp.ones((HG_CHUNK, HG_CHUNK), dtype=bool))[:, :, None]

    def step(state, inp):
        qc, kc, vc, lfc = inp
        b = jnp.cumsum(lfc, axis=2)
        o_inter = jnp.einsum('bhtk,bhkv->bhtv', qc * jnp.exp(b), state)
        diff = b[:, :, :, None, :] - b[:, :, None, :, :]
        decay = jnp.where(mask, jnp.exp(jnp.where(mask, diff, 0.0)), 0.0)
        scores = jnp.einsum('bhtk,bhtsk,bhsk->bhts', qc, decay, kc)
        o = o_inter + jnp.einsum('bhts,bhsv->bhtv', scores, vc)
        b_last = b[:, :, -1:, :]
        state = jnp.exp(b_last[:, :, 0, :])[..., None] * state + jnp.einsum('bhsk,bhsv->bhkv', kc * jnp.exp(b_last - b), vc)
        return state, o

    s0 = jnp.zeros((bsz, HG_HEADS, HG_HEAD_DIM, HG_HEAD_DIM), F32)
    _, o = lax.scan(step, s0, (qh, k, vh, log_f))
    o = o.transpose(1, 0, 3, 2, 4).reshape(bsz, L, HG_HEADS, HG_HEAD_DIM)
    o = rmsnorm(o, norm_g.reshape(HG_HEADS, HG_HEAD_DIM)).reshape(bsz, L, HG_WIDTH)
    return o * jax.nn.silu(gate.astype(F32))

def swiglu(h, w1, w3, w2):
    return (jax.nn.silu(h @ w1) * (h @ w3)) @ w2

def moe_swiglu(h, router, w1, w3, w2):
    T = h.shape[0]
    logits = h.astype(F32) @ router.astype(F32)
    top_val, top_idx = lax.top_k(logits, TOP_K)
    gates = jax.nn.softmax(top_val, axis=-1)
    flat_e = top_idx.reshape(-1)
    flat_tok = jnp.arange(T * TOP_K, dtype=jnp.int32) // TOP_K
    flat_g = gates.reshape(-1)
    order = jnp.argsort(flat_e)
    se, stok, sg = flat_e[order], flat_tok[order], flat_g[order]
    counts = jnp.zeros((N_EXPERTS,), jnp.int32).at[flat_e].add(1)
    padded = (counts + MOE_BLOCK - 1) // MOE_BLOCK * MOE_BLOCK
    start = jnp.cumsum(counts) - counts
    pend = jnp.cumsum(padded)
    pstart = pend - padded
    dest = pstart[se] + jnp.arange(T * TOP_K, dtype=jnp.int32) - start[se]
    n_blk = -(-(T * TOP_K) // MOE_BLOCK) + N_EXPERTS
    slot_tok = jnp.full((n_blk * MOE_BLOCK,), T, jnp.int32).at[dest].set(stok)
    slot_g = jnp.zeros((n_blk * MOE_BLOCK,), F32).at[dest].set(sg)
    blk_e = jnp.clip(jnp.searchsorted(pend, jnp.arange(n_blk, dtype=jnp.int32) * MOE_BLOCK, side='right'), 0, N_EXPERTS - 1)
    xs = jnp.take(h, slot_tok, axis=0, mode='fill', fill_value=0).reshape(n_blk, MOE_BLOCK, -1)

    def run_block(args):
        xb, e = args
        return swiglu(xb, w1[e], w3[e], w2[e])

    yb = lax.map(run_block, (xs, blk_e)).reshape(n_blk * MOE_BLOCK, -1)
    yb = yb * slot_g[:, None].astype(yb.dtype)
    return jnp.zeros_like(h).at[slot_tok].add(yb, mode='drop')

def setup_inputs(seed: int = 0) -> dict:
    key = jax.random.key(seed)
    ks = jax.random.split(key, 32)

    def nrm(k, shape, scale):
        return jax.random.normal(k, shape, F32) * scale

    def gain(k, shape):
        return 1.0 + 0.02 * jax.random.normal(k, shape, F32)

    return {
        "x": nrm(ks[0], (BATCH, SEQ, D_MODEL), 1.0),
        "attn_norm": gain(ks[1], (DEPTH, D_MODEL)),
        "ffn_norm": gain(ks[2], (DEPTH, D_MODEL)),
        "final_norm": gain(ks[3], (D_MODEL,)),
        "w_in": nrm(ks[4], (DEPTH, D_MODEL, D_IN), D_MODEL ** -0.5),
        "w_out": nrm(ks[5], (DEPTH, D_MIX, D_MODEL), D_MIX ** -0.5),
        "s5_lambda_re": -0.5 + 0.01 * jax.random.normal(ks[6], (DEPTH, S5_GROUPS, S5_STATE), F32),
        "s5_lambda_im": jnp.pi * jnp.arange(S5_STATE, dtype=F32) + 0.01 * jax.random.normal(ks[7], (DEPTH, S5_GROUPS, S5_STATE), F32),
        "s5_log_dt": jax.random.uniform(ks[8], (DEPTH, S5_GROUPS), F32, minval=math.log(DT_MIN), maxval=math.log(DT_MAX)),
        "s5_b_re": nrm(ks[9], (DEPTH, S5_GROUPS, S5_STATE, S5_GROUP), (2 * S5_GROUP) ** -0.5),
        "s5_b_im": nrm(ks[10], (DEPTH, S5_GROUPS, S5_STATE, S5_GROUP), (2 * S5_GROUP) ** -0.5),
        "s5_c_re": nrm(ks[11], (DEPTH, S5_GROUPS, S5_GROUP, S5_STATE), S5_STATE ** -0.5),
        "s5_c_im": nrm(ks[12], (DEPTH, S5_GROUPS, S5_GROUP, S5_STATE), S5_STATE ** -0.5),
        "s5_d": nrm(ks[13], (DEPTH, S5_WIDTH), 1.0),
        "s5_glu": nrm(ks[14], (DEPTH, S5_WIDTH, S5_WIDTH), S5_WIDTH ** -0.5),
        "s5_out_norm": gain(ks[15], (DEPTH, S5_WIDTH)),
        "conv_w": nrm(ks[16], (DEPTH, CONV_K, CONV_WIDTH), CONV_K ** -0.5),
        "conv_out_norm": gain(ks[17], (DEPTH, CONV_WIDTH)),
        "hg_lower_bounds": nrm(ks[18], (DEPTH, HG_WIDTH), 0.1),
        "hg_out_norm": gain(ks[19], (DEPTH, HG_WIDTH)),
        "ffn_w1": nrm(ks[20], (N_DENSE, D_MODEL, D_FF), D_MODEL ** -0.5),
        "ffn_w3": nrm(ks[21], (N_DENSE, D_MODEL, D_FF), D_MODEL ** -0.5),
        "ffn_w2": nrm(ks[22], (N_DENSE, D_FF, D_MODEL), D_FF ** -0.5),
        "moe_router": nrm(ks[23], (N_MOE, D_MODEL, N_EXPERTS), D_MODEL ** -0.5),
        "moe_w1": nrm(ks[24], (N_MOE, N_EXPERTS, D_MODEL, D_FF), D_MODEL ** -0.5),
        "moe_w3": nrm(ks[25], (N_MOE, N_EXPERTS, D_MODEL, D_FF), D_MODEL ** -0.5),
        "moe_w2": nrm(ks[26], (N_MOE, N_EXPERTS, D_FF, D_MODEL), D_FF ** -0.5),
    }

def reference(x, attn_norm, ffn_norm, final_norm, w_in, w_out,
              s5_lambda_re, s5_lambda_im, s5_log_dt, s5_b_re, s5_b_im, s5_c_re, s5_c_im,
              s5_d, s5_glu, s5_out_norm, conv_w, conv_out_norm, hg_lower_bounds, hg_out_norm,
              ffn_w1, ffn_w3, ffn_w2, moe_router, moe_w1, moe_w3, moe_w2):
    lb_soft = jax.nn.softmax(hg_lower_bounds.astype(F32), axis=0)
    lb_all = jnp.cumsum(lb_soft, axis=0) - lb_soft[0]
    h = x
    bsz, L, _ = x.shape
    for l in range(DEPTH):
        hn = rmsnorm(h, attn_norm[l])
        u, cb, cc, cv, hq, hf, hi, hgate = split_cols(hn @ w_in[l])
        y_s5 = s5_mixer(u, s5_lambda_re[l], s5_lambda_im[l], s5_log_dt[l], s5_b_re[l], s5_b_im[l],
                        s5_c_re[l], s5_c_im[l], s5_d[l], s5_glu[l])
        y_s5 = rmsnorm(y_s5, s5_out_norm[l])
        y_conv = rmsnorm(conv_mixer(cb, cc, cv, conv_w[l]), conv_out_norm[l])
        y_hg = hgrn2_mixer(hq, hf, hi, hgate, lb_all[l], hg_out_norm[l])
        mix = jnp.concatenate([y_s5.astype(h.dtype), y_conv.astype(h.dtype), y_hg.astype(h.dtype)], axis=-1)
        h = h + mix @ w_out[l]
        hn = rmsnorm(h, ffn_norm[l])
        j = l // 2
        if l % 2 == 0:
            ff = swiglu(hn, ffn_w1[j], ffn_w3[j], ffn_w2[j])
        else:
            ff = moe_swiglu(hn.reshape(bsz * L, D_MODEL), moe_router[j], moe_w1[j], moe_w3[j], moe_w2[j]).reshape(bsz, L, D_MODEL)
        h = h + ff
    return rmsnorm(h, final_norm)


_drawn_inputs = setup_inputs


def setup_inputs(seed=0):
    import zlib

    import numpy as np

    out = dict(_drawn_inputs(seed))
    spreads = {}
    factors = {'final_norm': 27.186,
     's5_lambda_re': 200.0,
     'conv_out_norm': 3.462,
     'hg_lower_bounds': 19.255,
     'ffn_norm': 3.037,
     's5_lambda_im': 13.358,
     's5_log_dt': 30.424,
     's5_b_re': 14.315,
     's5_b_im': 26.198,
     's5_c_re': 16.143,
     's5_c_im': 11.549,
     's5_out_norm': 4.299,
     'hg_out_norm': 4.534}
    for name, (base, spread) in spreads.items():
        noise = np.random.default_rng([zlib.crc32(name.encode()), seed]).standard_normal(out[name].shape)
        drawn = base * np.exp(spread * noise) if base else spread * noise
        out[name] = __import__('jax').numpy.asarray(drawn.astype(out[name].dtype))
    for name, factor in factors.items():
        out[name] = (out[name] * factor).astype(out[name].dtype)
    return out
```

```python
from contextlib import ExitStack

import concourse.bass as bass
from concourse import mybir

P = 128
T = 512
D = 1024
DK = D // P
DEPTH = 2
S5_G, S5_C, S5_N = 16, 16, 64
S5_T = 8
S5_NC = T // S5_T
PAIRS = S5_G // 2
HEADS = 4
CH = 128
NCH = T // CH
LEVELS = [64, 32, 16, 8, 4, 2, 1]
FF = 3584
FT = FF // P
GJ = 7
NG = FT // GJ
E = 8
A_SLOTS, B_SLOTS = 7, 4
A_W, B_W = DK * P, 2 * DK * P
W2_W = 2 * GJ * P
EVACS = 28
EPS = 1e-6
WIDTHS = (128, 160, 208, 512)

ALU = mybir.AluOpType
ACT = mybir.ActivationFunctionType
AX_X = mybir.AxisListType.X
F32 = mybir.dt.float32
I32 = mybir.dt.int32
U8 = mybir.dt.uint8

PARAMS = [("attn_norm", DK), ("ffn_norm", DK), ("final_norm", DK), ("lam_re", PAIRS), ("lam_im", PAIRS),
          ("log_dt", PAIRS), ("b_re", PAIRS * S5_C), ("b_im", PAIRS * S5_C), ("c_re", PAIRS * S5_C),
          ("c_im", PAIRS * S5_C), ("s5_d", 2), ("s5_norm", 2), ("conv_w", 6), ("conv_norm", 2),
          ("hg_norm", 4), ("lb0", 4), ("lb1", 4)]
PCOL, NPAR = {}, 0
for _n, _w in PARAMS:
    PCOL[_n] = (NPAR, NPAR + _w)
    NPAR += _w

CONSTS = [("ones", P), ("ident", P), ("before", P), ("tri8", 64), ("iota", T), ("scan", T), ("slot", 4), ("eps", 1),
          ("halfpi", 1)]
CCOL, NCON = {}, 0
for _n, _w in CONSTS:
    CCOL[_n] = (NCON, NCON + _w)
    NCON += _w

SEMS = """
par_in x_in const_in glu_in
squares sums rstd_ready xn_ready
u_proj proj_ready proj_evac
s5_dt s5_args s5_sin s5_w s5_wT s5_wT_evac s5_bc s5_k s5_k_evac s5_T_in
s5_us s5_u_out s5_u_in s5_v s5_x s5_y s5_y_evac s5_y_out s5_y_in s5_yd s5_gelu s5_glu s5_sig s5_sq s5_ssq s5_rstd
s5_mix conv_sq_in conv_ssq conv_rstd conv_z
lb_in lb_exp f_in f_ln b_diff b_exp b_mul score score_used tail_diff tail_exp tail_mul kdT kdT_evac kv states
head_o head_sq head_ssq head_rstd mix_ready
wout y_added
h1 w13 silu g_cnt y_ready y_cnt
xtok xtok_evac logits posT route_exp route_d route_done counts_ready sel_w sel_pos
sel_ready bc pos_bc G_ready gather gather_evac yT yT_evac scatter scatter_added
out_ready out_done
pe act dve pool
""".split()


def build(nc, x, win, wout, w13a, w2a, w13e, w2e, par, glu, router, const, masks, out):
    u_dram = nc.dram_tensor("u_dram", (DEPTH, 2, P, S5_T, S5_NC), F32, kind="Internal").ap()
    y_dram = nc.dram_tensor("y_dram", (DEPTH, S5_G, S5_C, S5_T, S5_NC), F32, kind="Internal").ap()

    with ExitStack() as ctx:
        def sb(name, shape, dt=F32):
            return ctx.enter_context(nc.sbuf_tensor(name, shape, dt))

        S = {n: ctx.enter_context(nc.semaphore(n)) for n in SEMS}
        a_full = [ctx.enter_context(nc.semaphore(f"a_full{i}")) for i in range(A_SLOTS)]
        b_full = [ctx.enter_context(nc.semaphore(f"b_full{i}")) for i in range(B_SLOTS)]
        bank = [ctx.enter_context(nc.psum_tensor(f"bank{i}", [P, T], F32)) for i in range(8)]

        h = sb("h", [P, DK, T])
        xn = sb("xn", [P, DK, T])
        A = sb("A", [P, A_SLOTS, A_W])
        B = sb("B", [P, B_SLOTS, B_W])
        parm = sb("parm", [P, DEPTH, NPAR])
        con = sb("con", [P, NCON])
        msk = sb("msk", [P, len(LEVELS) + 1, P], U8)
        glu_sb = sb("glu_sb", [P, DEPTH, 2, 256])
        rt_sb = sb("rt_sb", [P, DK, E])
        small = sb("small", [P, 64, PAIRS])
        pw = sb("pw", [P, 2, PAIRS, S5_T + 1])
        bb = sb("bb", [P, 2, PAIRS, S5_C])
        scr = sb("scr", [P, 24200])

        def cut(a, n):
            return scr[:, a:a + n]

        C = lambda n: con[:, CCOL[n][0]:CCOL[n][1]]
        PR = lambda l, n: parm[:, l, PCOL[n][0]:PCOL[n][1]]
        ones, ident = C("ones"), C("ident")
        eps = C("eps")
        ucv = cut(0, 4096).rearrange("p (m t) -> p m t", m=8)
        q = cut(4096, 2048).rearrange("p (h t) -> p h t", h=HEADS)
        f = cut(6144, 2048).rearrange("p (h t) -> p h t", h=HEADS)
        k = cut(8192, 2048).rearrange("p (h t) -> p h t", h=HEADS)
        gate = cut(10240, 2048).rearrange("p (h t) -> p h t", h=HEADS)
        v = cut(12288, 2048).rearrange("p (c d) -> p c d", c=NCH)
        EB = [cut(14336, 2048), cut(16384, 2048)]
        R3 = cut(18432, 2048)
        R4 = cut(20480, 2048)
        R5 = scr[:, 22528:24200]
        Tm = R3.rearrange("p (g m) -> p g m", g=S5_G)
        Bst = R4.rearrange("p (q r m) -> p q r m", q=PAIRS, r=2)
        CPn = PAIRS * (S5_T + 1) * S5_C
        cp = [cut(10240 + i * CPn, CPn).rearrange("p (q s c) -> p q s c", q=PAIRS, s=S5_T + 1) for i in range(2)]
        Wst = EB[0].rearrange("p (q r s c) -> p q r s c", q=PAIRS, r=2, s=S5_T)
        Wtmp = EB[1][:, 0:CPn]
        Kst = EB[1].rearrange("p (g m) -> p g m", g=S5_G)
        us = EB[0][:, 0:1024].rearrange("p (j s n) -> p j s n", j=2, s=S5_T)
        U = EB[0][:, 1024:2048].rearrange("p (g n) -> p g n", g=S5_G)
        X = R5[:, 0:1024].rearrange("p (r q n) -> p r q n", r=2, q=PAIRS)
        t1 = EB[1][:, 0:1024].rearrange("p (r q n) -> p r q n", r=2, q=PAIRS)
        t2 = EB[1][:, 1024:2048].rearrange("p (r q n) -> p r q n", r=2, q=PAIRS)
        Ysb = EB[1][:, 0:1024].rearrange("p (g n) -> p g n", g=S5_G)
        ych = EB[0][:, 0:1024].rearrange("p (j s n) -> p j s n", j=2, s=S5_T)
        yg = EB[1][:, 1024:2048].rearrange("p (j t) -> p j t", j=2)
        ysg = EB[0][:, 1024:2048].rearrange("p (j t) -> p j t", j=2)
        sq2 = R5[:, 0:1024].rearrange("p (j t) -> p j t", j=2)
        s5_rstd = R5[:, 1024:1536]
        sq = scr[:, 4096:4096 + DK * T].rearrange("p (m t) -> p m t", m=DK)
        rstd = scr[:, 8192:8192 + T]
        EV = [e.rearrange("p (h t) -> p h t", h=HEADS) for e in EB]
        PT = R3.rearrange("p (h t) -> p h t", h=HEADS)
        kdT = R4.rearrange("p (c h d) -> p c h d", c=NCH, h=HEADS)
        St = ucv[:, 0:3, :]
        dec = small[:, 60:62, :].rearrange("p a b -> p (a b)").rearrange("p (h c) -> p h c", h=HEADS)
        hsq = ucv[:, 3:5, :]
        hrs = ucv[:, 5:7, :]
        htmp = ucv[:, 7, :]
        g = cut(0, GJ * T).rearrange("p (j t) -> p j t", j=GJ)
        sil = cut(GJ * T, 3 * T).rearrange("p (j t) -> p j t", j=3)
        yt = cut(0, 4096).rearrange("p (s d) -> p s d", s=4)
        ye = cut(5120, 4096).rearrange("p (m t) -> p m t", m=DK)
        xtok = cut(9216, 4096).rearrange("p (i d) -> p i d", i=4)
        sel = cut(13312, 2048).rearrange("p (i t) -> p i t", i=4)
        G = cut(15360, 2048).rearrange("p (s t) -> p s t", s=4)
        rsm = cut(17408, 2048)
        posg = cut(19456, 1024).rearrange("p (r t) -> p r t", r=2)
        rv = lambda i, n=32: rsm[:, i * 64:i * 64 + n]
        lg = rv(0).rearrange("p (i e) -> p i e", i=4)
        cmp3 = rsm[:, 1024:1280].rearrange("p (i e f) -> p i e f", i=4, e=E)
        eq3 = rsm[:, 1280:1536].rearrange("p (i e f) -> p i e f", i=4, e=E)
        rank, selm, first, second = (rv(i).rearrange("p (i e) -> p i e", i=4) for i in (1, 2, 3, 4))
        top1, top2 = rv(5, 4), rv(6, 4)
        dlt, w2nd, w1st = rv(7, 4), rv(8, 4), rv(9, 4)
        gatem, posm = rv(10).rearrange("p (i e) -> p i e", i=4), rv(11).rearrange("p (i e) -> p i e", i=4)
        rtmp = rv(12).rearrange("p (i e) -> p i e", i=4)
        cnt_i = sb("cnt_i", [P, E], I32)
        omx = small[:, 48:52, :].rearrange("p a b -> p (a b)")
        lbm, oml = small[:, 52, 0:4], small[:, 53, 0:4]

        def chain(eng, s):
            n = [0]

            def link(ins):
                n[0] += 1
                ins.then_inc(s, 1)
                eng.wait_ge(s, n[0])
            link.count = n
            return link

        block = ctx.enter_context(nc.Block())

        @block.sync
        def _(sp):
            sp.dma_start(con[:], const).then_inc(S["const_in"], 16)
            for kk in range(DK):
                sp.dma_start(h[:, kk, :], x[kk]).then_inc(S["x_in"], 16)
            sp.dma_start(parm[:], par).then_inc(S["par_in"], 16)

            slot_tiles = [2, 4, 6, 8, 10, 12, 14, 16, 20, 24, 26, 28]

            def groups(l, w13_src, w2_src, gi, n):
                for i in range(2 * GJ):
                    sp.wait_ge(S["w13"], 2 * GJ * n + i + 1)
                    sp.dma_start(A[:, i % A_SLOTS, :], w13_src(gi, i)).then_inc(a_full[i % A_SLOTS], 16)
                for s in range(B_SLOTS):
                    if s == 0:
                        sp.wait_ge(S["wout"], DK * (l + 1))
                    sp.wait_ge(S["y_ready"], DK * n + 2 * s + 2)
                    sp.dma_start(B[:, s, 0:W2_W], w2_src(gi, s)).then_inc(b_full[s], 16)

            for l in range(DEPTH):
                for n in range(16):
                    if n >= B_SLOTS:
                        sp.wait_ge(S["proj_ready"], EVACS * l + slot_tiles[n - B_SLOTS])
                    elif l > 0:
                        sp.wait_ge(S["y_ready"], DK * NG + 2 * n + 2)
                    sp.dma_start(B[:, n % B_SLOTS, :], win[l, n] if n < 12 else wout[l, n - 12]
                                 ).then_inc(b_full[n % B_SLOTS], 16)
                    if l == 0 and n == 3:
                        sp.dma_start(R5[:, 0:(len(LEVELS) + 1) * P].rearrange("p (l t) -> p l t", t=P), masks
                                     ).then_inc(S["glu_in"], 16)
                        sp.dma_start(glu_sb[:], glu).then_inc(S["glu_in"], 16)
                        sp.dma_start(rt_sb[:], router).then_inc(S["glu_in"], 16)
                if l == 0:
                    with sp.Fori(0, NG) as gi:
                        groups(l, lambda a, i: w13a[bass.ds(a, 1), i].rearrange("a p c -> (a p) c"),
                               lambda a, s: w2a[bass.ds(a, 1), s].rearrange("a p c -> (a p) c"), gi, gi)
                else:
                    with sp.Fori(0, E * NG) as gi:
                        groups(l, lambda a, i: w13e[bass.ds(a, 1), i].rearrange("a p c -> (a p) c"),
                               lambda a, s: w2e[bass.ds(a, 1), s].rearrange("a p c -> (a p) c"), gi, gi + NG)
            for m in range(DK):
                sp.wait_ge(S["out_ready"], m + 1)
                sp.dma_start(out[m], sq[:, m, :]).then_inc(S["out_done"], 16)
            sp.wait_ge(S["out_done"], 16 * DK)

        @block.gpsimd
        def _(pool):
            link = chain(pool, S["pool"])
            for l in range(DEPTH):
                if l > 0:
                    pool.wait_ge(S["y_cnt"], 2 + DK * NG * l)
                    pool.wait_ge(S["squares"], DK * (2 * l + 1))
                link(nc.gpsimd.memset(R3, 0.0))
                pool.wait_ge(S["s5_k_evac"], 4 * (l + 1))
                for r in range(S5_T):
                    nc.gpsimd.dma_start(Tm[r * S5_C:(r + 1) * S5_C, :, (S5_T - 1 - r) * S5_C:P],
                                        Kst[0:S5_C, :, 0:(r + 1) * S5_C]).then_inc(S["s5_T_in"], 16)
                pool.wait_ge(S["s5_us"], l + 1)
                nc.gpsimd.dma_start(u_dram[l].rearrange("j p s n -> p j s n"), us).then_inc(S["s5_u_out"], 16)
                pool.wait_ge(S["s5_u_out"], 16 * (l + 1))
                for r in range(S5_T):
                    nc.gpsimd.dma_start(U[r * S5_C:(r + 1) * S5_C, :, :],
                                        u_dram[l, :, :, S5_T - 1 - r, :].rearrange("j (g c) n -> c (j g) n", c=S5_C)
                                        ).then_inc(S["s5_u_in"], 16)
                pool.wait_ge(S["s5_y_evac"], 2 * (l + 1))
                for t in range(S5_T):
                    for w in range(2):
                        nc.gpsimd.dma_start(
                            y_dram[l, :, :, t, :].rearrange("(q w) c n -> w c q n", w=2)[w],
                            Ysb[t * S5_C:(t + 1) * S5_C, w * PAIRS:(w + 1) * PAIRS, :]).then_inc(S["s5_y_out"], 16)
                pool.wait_ge(S["s5_y_out"], 2 * 16 * S5_T * (l + 1))
                nc.gpsimd.dma_start(ych, y_dram[l].rearrange("(j g) c s n -> (g c) j s n", j=2)
                                    ).then_inc(S["s5_y_in"], 16)

        @block.tensor
        def _(pe):
            mm = nc.tensor.matmul

            def norm_sums(n):
                for kk in range(DK):
                    pe.wait_ge(S["squares"], DK * n + kk + 1)
                    i = mm(bank[4][:], ones, sq[:, kk, :], start=(kk == 0), stop=(kk == DK - 1))
                i.then_inc(S["sums"], 1)

            def projection(l, idx, n_slot, first, tok=None):
                if EVACS * l + idx >= 4:
                    pe.wait_ge(S["proj_evac"], EVACS * l + idx - 3)
                s = n_slot % B_SLOTS
                if first:
                    pe.wait_ge(b_full[s], 16 * (n_slot // B_SLOTS + 1 + 8 * l))
                return s

            def channel_tiles(l, idx, slots):
                for n_slot in slots:
                    for m in range(2):
                        s = projection(l, idx, n_slot, m == 0)
                        for kk in range(DK):
                            i = mm(bank[idx % 4][:], B[:, s, (m * DK + kk) * P:(m * DK + kk + 1) * P], xn[:, kk, :],
                                   start=(kk == 0), stop=(kk == DK - 1))
                        i.then_inc(S["proj_ready"], 1)
                        idx += 1

            def value_tiles(l, idx, slots):
                for n_slot in slots:
                    for c in range(NCH):
                        s = projection(l, idx, n_slot, c == 0)
                        wv = B[:, s, :].rearrange("p (m k c) -> p k m c", m=2, k=DK)
                        for kk in range(DK):
                            i = mm(bank[idx % 4][:, 0:256], xn[:, kk, c * P:(c + 1) * P], wv[:, kk],
                                   start=(kk == 0), stop=(kk == DK - 1))
                        i.then_inc(S["proj_ready"], 1)
                        idx += 1

            def s5_matrices(l):
                pe.wait_ge(S["s5_w"], l + 1)
                for pr in range(PAIRS):
                    for r in range(2):
                        n = 2 * pr + r
                        i = nc.tensor.transpose(bank[4 + n // 4][:, (n % 4) * P:(n % 4 + 1) * P],
                                                Wst[:, pr, r].rearrange("p s c -> p (s c)"), ident)
                        if n % 4 == 3:
                            i.then_inc(S["s5_wT"], 1)
                pe.wait_ge(S["s5_bc"], l + 1)
                for gg in range(S5_G):
                    a, pr = 64 * (gg // PAIRS), gg % PAIRS
                    if gg % 4 == 0:
                        pe.wait_ge(S["s5_wT_evac"], 4 * l + gg // 4 + 1)
                    o = bank[4 + gg // 4][0:S5_C, (gg % 4) * P:(gg % 4 + 1) * P]
                    for r in range(2):
                        i = mm(o, bb[a:a + 64, r, pr, :], cp[r][a:a + 64, pr, 0:S5_T, :].rearrange("p s c -> p (s c)"),
                               start=(r == 0), stop=(r == 1))
                    if gg % 4 == 3:
                        i.then_inc(S["s5_k"], 1)

            def s5_in(l):
                pe.wait_ge(S["s5_k_evac"], 4 * (l + 1))
                pe.wait_ge(S["s5_u_in"], 16 * S5_T * (l + 1))
                for r in range(2):
                    for gg in range(S5_G):
                        a, pr = 64 * (gg % 2), gg // 2
                        i = mm(bank[4 + r][a:a + 64, pr * S5_NC:(pr + 1) * S5_NC], Bst[:, pr, r, a:a + 64],
                               U[:, gg, :], start=True, stop=True)
                i.then_inc(S["s5_v"], 1)

            def s5_out(l):
                pe.wait_ge(S["s5_T_in"], 16 * S5_T * (l + 1))
                pe.wait_ge(S["s5_x"], l + 1)
                for gg in range(S5_G):
                    a, pr = 64 * (gg // PAIRS), gg % PAIRS
                    o = bank[6 + gg // PAIRS]
                    c0 = pr * S5_NC
                    mm(o[:, c0:c0 + S5_NC], Tm[:, gg, :], U[:, 2 * pr + gg // PAIRS, :], start=True, stop=False)
                    for r in range(2):
                        i = mm(o[:, c0 + 1:c0 + S5_NC],
                               cp[r][a:a + 64, pr, 1:S5_T + 1, :].rearrange("p s c -> p (s c)"),
                               X[a:a + 64, r, pr, 0:S5_NC - 1], start=False, stop=(r == 1))
                    if gg % 8 == 7:
                        i.then_inc(S["s5_y"], 1)

            def s5_glu(l):
                pe.wait_ge(S["s5_gelu"], l + 1)
                for m in range(2):
                    for kk in range(2):
                        i = mm(bank[4 + m][:], glu_sb[:, l, kk, m * P:(m + 1) * P], yg[:, kk, :],
                               start=(kk == 0), stop=(kk == 1))
                i.then_inc(S["s5_glu"], 1)

            def s5_norm(l):
                pe.wait_ge(S["s5_sq"], l + 1)
                for m in range(2):
                    i = mm(bank[6][:], ones, sq2[:, m, :], start=(m == 0), stop=(m == 1))
                i.then_inc(S["s5_ssq"], 1)

            def conv_norm(l):
                pe.wait_ge(S["conv_sq_in"], l + 1)
                for m in range(2):
                    i = mm(bank[7][:], ones, ucv[:, 4 + m, :], start=(m == 0), stop=(m == 1))
                i.then_inc(S["conv_ssq"], 1)

            def hgrn(l):
                n_lv = len(LEVELS)
                for li in range(n_lv + 1):
                    if li < n_lv:
                        pe.wait_ge(S["b_mul"], n_lv * l + li + 1)
                    for hh in range(HEADS):
                        done = (n_lv + 1) * HEADS * l + HEADS * (li - 2) + hh + 1
                        if li >= 2:
                            pe.wait_ge(S["score_used"], done)
                        for c in range(NCH):
                            lhs = EV[li % 2][:, hh, c * CH:(c + 1) * CH] if li < n_lv else k[:, hh, c * CH:(c + 1) * CH]
                            rhs = lhs if li < n_lv else q[:, hh, c * CH:(c + 1) * CH]
                            i = mm(bank[hh + 4 * (li % 2)][:, c * CH:(c + 1) * CH], lhs, rhs, start=True, stop=True)
                        i.then_inc(S["score"], 1)
                pe.wait_ge(S["tail_mul"], 2 * l + 2)
                pe.wait_ge(S["score_used"], (n_lv + 1) * HEADS * (l + 1))
                for c in range(NCH):
                    for hh in range(HEADS):
                        i = nc.tensor.transpose(bank[4 + c][:, hh * P:(hh + 1) * P], EV[1][:, hh, c * CH:(c + 1) * CH],
                                                ident)
                    i.then_inc(S["kdT"], 1)
                for c in range(NCH - 1):
                    pe.wait_ge(S["kdT_evac"], NCH * l + c + 1)
                    for hh in range(HEADS):
                        i = mm(bank[4 + c][:, hh * P:(hh + 1) * P], kdT[:, c, hh, :], v[:, c, hh * P:(hh + 1) * P],
                               start=True, stop=True)
                    i.then_inc(S["kv"], 1)
                for hh in range(HEADS):
                    for c in range(NCH):
                        if c > 0 and hh == 0:
                            pe.wait_ge(S["states"], 3 * l + c)
                        o = bank[hh][:, c * CH:(c + 1) * CH]
                        i = mm(o, v[:, c, hh * P:(hh + 1) * P], PT[:, hh, c * CH:(c + 1) * CH],
                               start=True, stop=(c == 0))
                        if c > 0:
                            i = mm(o, St[:, c - 1, hh * P:(hh + 1) * P], EV[0][:, hh, c * CH:(c + 1) * CH],
                                   start=False, stop=True)
                    i.then_inc(S["head_o"], 1)
                pe.wait_ge(S["kdT_evac"], NCH * (l + 1))
                for hh in range(HEADS):
                    pe.wait_ge(S["head_sq"], HEADS * l + hh + 1)
                    mm(bank[4 + hh][:], ones, hsq[:, hh % 2, :], start=True, stop=True).then_inc(S["head_ssq"], 1)

            def out_projection(l):
                for m in range(DK):
                    s = (m // 2) % B_SLOTS
                    if m == 0:
                        pe.wait_ge(S["mix_ready"], 6 * (l + 1))
                    if m % 2 == 0:
                        pe.wait_ge(b_full[s], 16 * (4 + 8 * l))
                    if m >= 2:
                        pe.wait_ge(S["y_added"], DK * l + m - 1)
                    for kk in range(DK):
                        i = mm(bank[m % 2][:], B[:, s, ((m % 2) * DK + kk) * P:((m % 2) * DK + kk + 1) * P],
                               xn[:, kk, :], start=(kk == 0), stop=(kk == DK - 1))
                    i.then_inc(S["wout"], 1)

            PAIR = [0, 1, 0, 1, 0, 1, 2]
            LAST = [-3, -2, 0, 1, 2, 3, -1]

            def ffn_group(n, first_use, W, e=None):
                if e is not None:
                    pe.wait_ge(S["gather_evac"], DK * e + DK)
                for j in range(GJ):
                    b = 2 * PAIR[j]
                    pe.wait_ge(S["g_cnt"], GJ * n + (GJ + LAST[j] if LAST[j] >= 0 else GJ + LAST[j]) + 1)
                    for w in range(2):
                        i_a = 2 * j + w
                        pe.wait_ge(a_full[i_a % A_SLOTS], 32 * n + 16 * (i_a // A_SLOTS + 1))
                        for kk in range(DK):
                            i = mm(bank[b + w][:, 0:W], A[:, i_a % A_SLOTS, kk * P:(kk + 1) * P], xn[:, kk, 0:W],
                                   start=(kk == 0), stop=(kk == DK - 1))
                        i.then_inc(S["w13"], 1)
                for m in range(DK):
                    s = m // 2
                    if m % 2 == 0:
                        pe.wait_ge(b_full[s], 16 * n + 16 * (first_use + 1))
                    pe.wait_ge(S["y_cnt"], DK * n + m + 1)
                    for j in range(GJ):
                        if m == 0:
                            pe.wait_ge(S["g_cnt"], GJ * n + GJ + j + 1)
                        i = mm(bank[6 + m % 2][:, 0:W], B[:, s, ((m % 2) * GJ + j) * P:((m % 2) * GJ + j + 1) * P],
                               g[:, j, 0:W], start=(j == 0), stop=(j == GJ - 1))
                    i.then_inc(S["y_ready"], 1)

            def route():
                for i4 in range(4):
                    for kk in range(DK):
                        i = mm(bank[0][:, i4 * E:(i4 + 1) * E], xn[:, kk, i4 * P:(i4 + 1) * P], rt_sb[:, kk, :],
                               start=(kk == 0), stop=(kk == DK - 1))
                i.then_inc(S["logits"], 1)
                for i4 in range(4):
                    for half in range(2):
                        n = 2 * i4 + half
                        if n >= 4:
                            pe.wait_ge(S["xtok_evac"], n - 3)
                        for c in range(4):
                            i = nc.tensor.transpose(bank[4 + n % 4][:, c * P:(c + 1) * P],
                                                    xn[:, 4 * half + c, i4 * P:(i4 + 1) * P], ident)
                        i.then_inc(S["xtok"], 1)
                pe.wait_ge(S["route_d"], 1)
                for i4 in range(4):
                    for j4 in range(i4 + 1):
                        mm(bank[1][:, i4 * E:(i4 + 1) * E], C("before") if j4 == i4 else ones, selm[:, j4, :],
                           start=(j4 == 0), stop=(j4 == i4))
                for j4 in range(4):
                    i = mm(bank[1][:, 4 * E:5 * E], ones, selm[:, j4, :], start=(j4 == 0), stop=(j4 == 3))
                i.then_inc(S["posT"], 1)

            def spread(e):
                pe.wait_ge(S["sel_pos"], e + 1)
                for r in range(2):
                    for i4 in range(4):
                        i = mm(bank[4 + r][:, i4 * P:(i4 + 1) * P],
                               posg[:, r, i4 * P:(i4 + 1) * P], ident, start=True, stop=True)
                i.then_inc(S["bc"], 1)

            def expert(e, W):
                pe.wait_ge(S["sel_ready"], e + 1)
                for m in range(DK):
                    if m >= 2:
                        pe.wait_ge(S["gather_evac"], DK * e + m - 1)
                    for i4 in range(4):
                        i = mm(bank[m % 2][:, 0:W], xtok[:, i4, m * P:(m + 1) * P], sel[:, i4, 0:W],
                               start=(i4 == 0), stop=(i4 == 3))
                    i.then_inc(S["gather"], 1)
                with pe.Fori(0, NG) as gi:
                    ffn_group(e * NG + gi + NG, 12 - NG, W, e)
                pe.wait_ge(S["y_cnt"], DK * NG * e + DK * 2 * NG + 2)
                tiles = [(s, min(P, W - s * P)) for s in range((W + P - 1) // P)]
                for s, rows in tiles:
                    for half in range(2):
                        n = 2 * s + half
                        if n >= 4:
                            pe.wait_ge(S["yT_evac"], 8 * e + n - 3)
                        for c in range(4):
                            i = nc.tensor.transpose(bank[n % 4][0:rows, c * P:(c + 1) * P],
                                                    ye[:, 4 * half + c, s * P:s * P + rows], ident)
                        i.then_inc(S["yT"], 9 - 2 * len(tiles) if n == 2 * len(tiles) - 1 else 1)
                pe.wait_ge(S["yT_evac"], 8 * e + 8)
                pe.wait_ge(S["G_ready"], e + 1)
                for m in range(DK):
                    if m >= 2:
                        pe.wait_ge(S["scatter_added"], DK * e + m - 1)
                    for s, rows in tiles:
                        i = mm(bank[4 + m % 2][:], yt[0:rows, s, m * P:(m + 1) * P], G[0:rows, s, :],
                               start=(s == 0), stop=(s == len(tiles) - 1))
                    i.then_inc(S["scatter"], 1)
                pe.wait_ge(S["scatter_added"], DK * e + DK)

            pe.wait_ge(S["const_in"], 16)
            pe.nop().then_inc(S["w13"], A_SLOTS)
            pe.nop().then_inc(S["y_ready"], DK)
            for l in range(DEPTH):
                norm_sums(2 * l)
                for kk in range(DK):
                    pe.wait_ge(S["xn_ready"], DK * 2 * l + kk + 1)
                channel_tiles(l, 0, range(0, 4))
                s5_matrices(l)
                channel_tiles(l, 8, range(4, 6))
                s5_in(l)
                channel_tiles(l, 12, range(6, 8))
                s5_out(l)
                if l == 0:
                    pe.wait_ge(S["glu_in"], 48)
                value_tiles(l, 16, range(8, 10))
                s5_glu(l)
                channel_tiles(l, 24, range(10, 12))
                conv_norm(l)
                s5_norm(l)
                pe.wait_ge(S["proj_evac"], EVACS * (l + 1))
                pe.wait_ge(S["conv_rstd"], l + 1)
                pe.wait_ge(S["s5_rstd"], l + 1)
                pe.wait_ge(S["s5_sig"], l + 1)
                hgrn(l)
                out_projection(l)
                norm_sums(2 * l + 1)
                for kk in range(DK):
                    pe.wait_ge(S["xn_ready"], DK * (2 * l + 1) + kk + 1)
                if l == 0:
                    with pe.Fori(0, NG) as gi:
                        ffn_group(gi, 4, T)
                else:
                    route()
                    pe.wait_ge(S["xtok_evac"], 8)
                    pe.wait_ge(S["counts_ready"], 1)
                    with pe.Fori(0, E) as e:
                        spread(e)
                        n_tok = pe.value_load(cnt_i[0:1, bass.ds(e, 1)], min_val=0, max_val=T)

                        def choose(ws):
                            if len(ws) == 1:
                                expert(e, ws[0])
                                return
                            with pe.If(n_tok <= ws[0]):
                                expert(e, ws[0])
                            with pe.Else():
                                choose(ws[1:])
                                pe.nop()
                        choose(list(WIDTHS))
                    norm_sums(2 * DEPTH)

        @block.scalar
        def _(act):
            fn = nc.scalar.activation
            link = chain(act, S["act"])

            def norm_rstd(s_wait, n, ps, dst, width, s_done):
                act.wait_ge(S[s_wait], n)
                link(fn(dst, ps, ACT.Ln, bias=eps, scale=1.0 / width))
                fn(dst, dst, ACT.Exp, scale=-0.5).then_inc(S[s_done], 1)

            def evac(l, idx, dst, func=ACT.Copy, cols=T, inc=True, scale=1.0):
                act.wait_ge(S["proj_ready"], EVACS * l + idx + 1)
                i = fn(dst, bank[idx % 4][:, 0:cols], func, scale=scale)
                if inc:
                    i.then_inc(S["proj_evac"], 1)

            def mixers(l):
                if l > 0:
                    act.wait_ge(S["s5_mix"], l)
                act.wait_ge(S["par_in"], 16)
                fn(small[:, 0, :], PR(l, "log_dt"), ACT.Exp).then_inc(S["s5_dt"], 1)
                act.wait_ge(S["s5_args"], l + 1)
                fn(small[:, 3, :], small[:, 1, :], ACT.Exp)
                fn(small[:, 5, :], small[:, 4, :], ACT.Sin)
                fn(small[:, 7, :], small[:, 6, :], ACT.Sin).then_inc(S["s5_sin"], 1)
                act.wait_ge(S["lb_in"], l + 1)
                fn(omx[:, 8:16], omx[:, 0:8], ACT.Exp).then_inc(S["lb_exp"], 1)
                for i in range(8):
                    evac(l, i, ucv[:, i, :])
                for i in range(4):
                    act.wait_ge(S["s5_wT"], 4 * l + i + 1)
                    fn(R4[:, i * T:(i + 1) * T], bank[4 + i][:], ACT.Copy).then_inc(S["s5_wT_evac"], 1)
                for i in range(4):
                    act.wait_ge(S["s5_k"], 4 * l + i + 1)
                    if i == 0:
                        act.wait_ge(S["s5_bc"], l + 1)
                    fn(Kst[0:S5_C].rearrange("p g m -> p (g m)")[:, i * T:(i + 1) * T], bank[4 + i][0:S5_C, :],
                       ACT.Copy).then_inc(S["s5_k_evac"], 1)
                for i in range(4):
                    evac(l, 8 + i, f[:, i, :], ACT.Sigmoid, inc=False)
                    evac(l, 8 + i, k[:, i, :], ACT.Sigmoid, scale=-1.0)
                for i in range(4):
                    evac(l, 12 + i, q[:, i, :], ACT.Silu)
                for i in range(2):
                    act.wait_ge(S["s5_y"], 2 * l + i + 1)
                    if i == 0:
                        act.wait_ge(S["s5_x"], l + 1)
                    fn(Ysb[:, 8 * i:8 * i + 8, :].rearrange("p g n -> p (g n)"), bank[6 + i][:],
                       ACT.Copy).then_inc(S["s5_y_evac"], 1)
                for n in range(2):
                    for c in range(NCH):
                        evac(l, 16 + 4 * n + c, v[:, c, n * 256:(n + 1) * 256], cols=256)
                act.wait_ge(S["s5_yd"], l + 1)
                fn(yg, yg, ACT.Gelu_apprx_tanh).then_inc(S["s5_gelu"], 1)
                for i in range(4):
                    evac(l, 24 + i, gate[:, i, :], ACT.Silu)
                act.wait_ge(S["s5_glu"], l + 1)
                for m in range(2):
                    i = fn(ysg[:, m, :], bank[4 + m][:], ACT.Sigmoid)
                i.then_inc(S["s5_sig"], 1)
                norm_rstd("conv_ssq", l + 1, bank[7][:], ucv[:, 1, :], 256, "conv_rstd")
                norm_rstd("s5_ssq", l + 1, bank[6][:], s5_rstd, 256, "s5_rstd")
                act.wait_ge(S["f_in"], l + 1)
                fn(f, f, ACT.Ln)
                fn(EV[0], EV[0], ACT.Ln).then_inc(S["f_ln"], 1)
                for li in range(len(LEVELS)):
                    act.wait_ge(S["b_diff"], len(LEVELS) * l + li + 1)
                    fn(EB[li % 2], EB[li % 2], ACT.Exp).then_inc(S["b_exp"], 1)
                act.wait_ge(S["tail_diff"], 2 * l + 1)
                fn(dec, f.rearrange("p h (c t) -> p h c t", c=NCH)[:, :, :, CH - 1], ACT.Exp)
                fn(EV[0], f, ACT.Exp).then_inc(S["tail_exp"], 1)
                act.wait_ge(S["tail_diff"], 2 * l + 2)
                fn(EB[1], EB[1], ACT.Exp).then_inc(S["tail_exp"], 1)
                for c in range(NCH):
                    act.wait_ge(S["kdT"], NCH * l + c + 1)
                    fn(kdT[:, c].rearrange("p h d -> p (h d)"), bank[4 + c][:], ACT.Copy).then_inc(S["kdT_evac"], 1)
                for hh in range(HEADS):
                    act.wait_ge(S["head_o"], HEADS * l + hh + 1)
                    if hh >= 2:
                        act.wait_ge(S["head_ssq"], HEADS * l + hh - 1)
                    fn(hsq[:, hh % 2, :], bank[hh][:], ACT.Square).then_inc(S["head_sq"], 1)
                for hh in range(HEADS):
                    if hh >= 2:
                        act.wait_ge(S["mix_ready"], 6 * l + 2 + hh - 1)
                    norm_rstd("head_ssq", HEADS * l + hh + 1, bank[4 + hh][:], hrs[:, hh % 2, :], P, "head_rstd")

            SIL = [0, 1, 0, 1, 0, 1, 2]
            LAST = [-3, -2, 0, 1, 2, 3, -1]

            def ffn_silu(n):
                for j in range(GJ):
                    act.wait_ge(S["w13"], 2 * GJ * n + A_SLOTS + 2 * j + 1)
                    act.wait_ge(S["g_cnt"], GJ * n + GJ + LAST[j] + 1)
                    fn(sil[:, SIL[j], :], bank[2 * SIL[j]][:], ACT.Silu).then_inc(S["silu"], 1)

            def norm_of_h(n):
                norm_rstd("sums", n + 1, bank[4][:], rstd, D, "rstd_ready")

            act.wait_ge(S["const_in"], 16)
            for l in range(DEPTH):
                norm_of_h(2 * l)
                mixers(l)
                norm_of_h(2 * l + 1)
                if l == 0:
                    with act.Fori(0, NG) as gi:
                        ffn_silu(gi)
            for n in range(8):
                act.wait_ge(S["xtok"], n + 1)
                fn(xtok[:, n // 2, (n % 2) * T:(n % 2 + 1) * T], bank[4 + n % 4][:], ACT.Copy
                   ).then_inc(S["xtok_evac"], 1)
            act.wait_ge(S["route_exp"], 1)
            fn(w2nd, dlt, ACT.Exp).then_inc(S["route_exp"], 1)
            with act.Fori(0, E) as e:
                act.wait_ge(S["bc"], e + 1)
                for m in range(DK):
                    act.wait_ge(S["gather"], DK * e + m + 1)
                    fn(xn[:, m, :], bank[m % 2][:], ACT.Copy).then_inc(S["gather_evac"], 1)
                with act.Fori(0, NG) as gi:
                    ffn_silu(e * NG + gi + NG)
                for n in range(8):
                    act.wait_ge(S["yT"], 8 * e + n + 1)
                    fn(yt[:, n // 2, (n % 2) * T:(n % 2 + 1) * T], bank[n % 4][:], ACT.Copy
                       ).then_inc(S["yT_evac"], 1)
            norm_of_h(2 * DEPTH)

        @block.vector
        def _(dve):
            V = nc.vector
            link = chain(dve, S["dve"])
            tt, ts, stt = V.tensor_tensor, V.tensor_scalar, V.scalar_tensor_tensor
            MUL, ADD, SUB = ALU.mult, ALU.add, ALU.subtract

            def norm_of_h(n, gain, dst, done):
                for kk in range(DK):
                    if n == 0:
                        dve.wait_ge(S["x_in"], 16 * DK)
                    tt(sq[:, kk, :], h[:, kk, :], h[:, kk, :], MUL).then_inc(S["squares"], 1)
                dve.wait_ge(S["rstd_ready"], n + 1)
                for kk in range(DK):
                    stt(dst[:, kk, :], h[:, kk, :], gain[:, kk:kk + 1], rstd, MUL, MUL).then_inc(S[done], 1)

            def s5_discretise(l):
                sm = lambda i: small[:, i, :]
                dve.wait_ge(S["s5_dt"], l + 1)
                tt(sm(1), PR(l, "lam_re"), sm(0), MUL)
                link(tt(sm(2), PR(l, "lam_im"), sm(0), MUL))
                import math
                magic = 1.5 * 2.0 ** 23
                link(ts(sm(8), sm(2), 1.0 / (2 * math.pi), magic, MUL, ADD))
                link(ts(sm(8), sm(8), magic, None, SUB))
                for part in (6.28125, 0.0019350051879882812, 3.0199159819e-07):
                    link(stt(sm(2), sm(8), -part, sm(2), MUL, ADD))
                link(ts(sm(4), sm(2), math.pi * (1 - 1e-7), -math.pi * (1 - 1e-7), ALU.min, ALU.max))
                link(ts(sm(6), sm(4), -1.0, None, MUL))
                link(tt(sm(6), sm(6), sm(4), ALU.max))
                ts(sm(6), sm(6), -1.0, math.pi / 2, MUL, ADD).then_inc(S["s5_args"], 1)
                dve.wait_ge(S["s5_sin"], l + 1)
                pr_, pi_ = pw[:, 0], pw[:, 1]
                link(V.memset(pr_[:, :, 0], 1.0))
                link(V.memset(pi_[:, :, 0], 0.0))
                link(tt(pr_[:, :, 1], sm(3), sm(7), MUL))
                link(tt(pi_[:, :, 1], sm(3), sm(5), MUL))

                def powers(a, n, by):
                    src = lambda r: pw[:, r, :, a:a + n]
                    mul = lambda r: pw[:, r, :, by:by + 1].to_broadcast([P, PAIRS, n])
                    dst = lambda r: pw[:, r, :, a + by:a + by + n]
                    tmp = lambda i: small[:, 16 + 4 * i:20 + 4 * i, :].rearrange("p a q -> p (a q)")[
                        :, 0:PAIRS * n].rearrange("p (q n) -> p q n", n=n)
                    tt(tmp(0), src(0), mul(0), MUL)
                    tt(tmp(1), src(1), mul(1), MUL)
                    tt(tmp(2), src(0), mul(1), MUL)
                    link(tt(tmp(3), src(1), mul(0), MUL))
                    tt(dst(0), tmp(0), tmp(1), SUB)
                    link(tt(dst(1), tmp(2), tmp(3), ADD))
                powers(1, 1, 1)
                powers(1, 2, 2)
                powers(1, 4, 4)
                link(ts(sm(9), pr_[:, :, 1], 1.0, None, SUB))
                lr, li_ = PR(l, "lam_re"), PR(l, "lam_im")
                tt(sm(10), lr, lr, MUL)
                link(tt(sm(11), li_, li_, MUL))
                link(tt(sm(10), sm(10), sm(11), ADD))
                link(V.reciprocal(sm(10), sm(10)))
                tt(sm(11), sm(9), lr, MUL)
                tt(sm(12), pi_[:, :, 1], li_, MUL)
                tt(sm(13), pi_[:, :, 1], lr, MUL)
                link(tt(sm(14), sm(9), li_, MUL))
                tt(sm(11), sm(11), sm(12), ADD)
                link(tt(sm(13), sm(13), sm(14), SUB))
                tt(sm(11), sm(11), sm(10), MUL)
                link(tt(sm(13), sm(13), sm(10), MUL))
                v3 = lambda n: PR(l, n).rearrange("p (q c) -> p q c", q=PAIRS)
                br, bi, cr, ci = v3("b_re"), v3("b_im"), v3("c_re"), v3("c_im")
                bc = lambda a: a.unsqueeze(2).to_broadcast([P, PAIRS, S5_C])
                tq = [Wtmp[:, i * P:(i + 1) * P].rearrange("p (q c) -> p q c", q=PAIRS) for i in range(4)]
                tt(tq[0], br, bc(sm(11)), MUL)
                tt(tq[1], bi, bc(sm(13)), MUL)
                tt(tq[2], br, bc(sm(13)), MUL)
                link(tt(tq[3], bi, bc(sm(11)), MUL))
                tt(bb[:, 0], tq[0], tq[1], SUB)
                link(tt(bb[:, 1], tq[2], tq[3], ADD))
                n = S5_T
                shape = [P, PAIRS, n, S5_C]
                pb = lambda r, n: pw[:, r, :, 0:n].unsqueeze(3).to_broadcast([P, PAIRS, n, S5_C])
                b4 = lambda a, n: a.unsqueeze(2).to_broadcast([P, PAIRS, n, S5_C])
                w4 = lambda n: Wtmp[:, 0:PAIRS * n * S5_C].rearrange("p (q s c) -> p q s c", q=PAIRS, s=n)
                link(tt(Wst[:, :, 0], pb(0, n), b4(bb[:, 0], n), MUL))
                link(tt(w4(n), pb(1, n), b4(bb[:, 1], n), MUL))
                link(tt(Wst[:, :, 0], Wst[:, :, 0], w4(n), SUB))
                link(tt(Wst[:, :, 1], pb(0, n), b4(bb[:, 1], n), MUL))
                link(tt(w4(n), pb(1, n), b4(bb[:, 0], n), MUL))
                tt(Wst[:, :, 1], Wst[:, :, 1], w4(n), ADD).then_inc(S["s5_w"], 1)
                dve.wait_ge(S["s5_w"], l + 1)
                n = S5_T + 1
                link(tt(cp[0], pb(0, n), b4(cr, n), MUL))
                link(tt(w4(n), pb(1, n), b4(ci, n), MUL))
                link(tt(cp[0], cp[0], w4(n), SUB))
                link(tt(cp[1], pb(1, n), b4(cr, n), MUL))
                link(tt(w4(n), pb(0, n), b4(ci, n), MUL))
                stt(cp[1], cp[1], -1.0, w4(n), MUL, SUB).then_inc(S["s5_bc"], 1)

            def hgrn_bounds(l):
                a0, a1 = PR(0, "lb0"), PR(0, "lb1")
                link(tt(omx[:, 16:20], a0, a1, ALU.max))
                tt(omx[:, 0:4], a0, omx[:, 16:20], SUB)
                tt(omx[:, 4:8], a1, omx[:, 16:20], SUB).then_inc(S["lb_in"], 1)
                dve.wait_ge(S["lb_exp"], l + 1)
                link(tt(omx[:, 20:24], omx[:, 8:12], omx[:, 12:16], ADD))
                link(V.reciprocal(omx[:, 20:24], omx[:, 20:24]))
                tt(omx[:, 24:28], omx[:, 8:12], omx[:, 20:24], MUL)
                link(tt(omx[:, 28:32], omx[:, 12:16], omx[:, 20:24], MUL))
                if l == 0:
                    link(tt(lbm, omx[:, 24:28], omx[:, 24:28], SUB))
                else:
                    link(tt(lbm, omx[:, 24:28], omx[:, 28:32], ADD))
                    link(tt(lbm, lbm, omx[:, 24:28], SUB))
                link(ts(lbm, lbm, 0.0, 1.0 - 1e-6, ALU.max, ALU.min))
                link(ts(oml, lbm, -1.0, 1.0, MUL, ADD))
                link(ts(lbm, lbm, 1e-30, None, ALU.max))

            def conv(l):
                w = PR(l, "conv_w")
                dve.wait_ge(S["proj_evac"], EVACS * l + 8)
                for m in range(2):
                    gb, z, vv = ucv[:, 2 + m, :], ucv[:, 4 + m, :], ucv[:, 6 + m, :]
                    link(tt(z, z, vv, MUL))
                    col = lambda tap: w[:, 2 * tap + m:2 * tap + m + 1]
                    link(ts(vv, z, col(2), None, MUL))
                    link(stt(vv[:, 1:T], z[:, 0:T - 1], col(1), vv[:, 1:T], MUL, ADD))
                    link(stt(vv[:, 2:T], z[:, 0:T - 2], col(0), vv[:, 2:T], MUL, ADD))
                    link(tt(vv, vv, gb, MUL))
                    i = tt(z, vv, vv, MUL)
                    if m == 0:
                        link(i)
                    else:
                        i.then_inc(S["conv_sq_in"], 1)

            def s5_rows(l):
                dve.wait_ge(S["s5_wT"], 4 * (l + 1))
                for j in range(2):
                    i = V.tensor_copy(us[:, j], ucv[:, j, :].rearrange("p (n s) -> p s n", s=S5_T))
                    if j == 0:
                        link(i)
                i.then_inc(S["s5_us"], 1)

            def s5_scan(l):
                dve.wait_ge(S["s5_v"], l + 1)
                dve.wait_ge(S["s5_T_in"], 16 * S5_T * (l + 1))
                for r in range(2):
                    i = V.tensor_copy(X[:, r].rearrange("p q n -> p (q n)"), bank[4 + r][:])
                link(i)
                a = lambda i: small[:, 32 + i, :]
                V.tensor_copy(a(0), pw[:, 0, :, S5_T])
                link(V.tensor_copy(a(1), pw[:, 1, :, S5_T]))
                d = 1
                while d < S5_NC:
                    n = S5_NC - d
                    for r in range(2):
                        src = X[:, r, :, 0:n]
                        tt(t1[:, r, :, 0:n], src, a(0).unsqueeze(2).to_broadcast([P, PAIRS, n]), MUL)
                        i = tt(t2[:, r, :, 0:n], src, a(1).unsqueeze(2).to_broadcast([P, PAIRS, n]), MUL)
                    link(i)
                    for r in range(2):
                        i = tt(X[:, r, :, d:], X[:, r, :, d:], t1[:, r, :, 0:n], ADD)
                    link(i)
                    tt(X[:, 0, :, d:], X[:, 0, :, d:], t2[:, 1, :, 0:n], SUB)
                    i = tt(X[:, 1, :, d:], X[:, 1, :, d:], t2[:, 0, :, 0:n], ADD)
                    d *= 2
                    if d < S5_NC:
                        link(i)
                        tt(a(2), a(0), a(0), MUL)
                        tt(a(3), a(1), a(1), MUL)
                        link(tt(a(4), a(0), a(1), MUL))
                        tt(a(0), a(2), a(3), SUB)
                        link(ts(a(1), a(4), 2.0, None, MUL))
                    else:
                        i.then_inc(S["s5_x"], 1)

            def s5_tail(l):
                dve.wait_ge(S["s5_y_in"], 16 * (l + 1))
                for j in range(2):
                    i = stt(yg[:, j, :].rearrange("p (n s) -> p n s", s=S5_T),
                            ucv[:, j, :].rearrange("p (n s) -> p n s", s=S5_T), PR(l, "s5_d")[:, j:j + 1],
                            ych[:, j].rearrange("p s n -> p n s"), MUL, ADD)
                    if j == 0:
                        link(i)
                i.then_inc(S["s5_yd"], 1)
                dve.wait_ge(S["s5_sig"], l + 1)
                link(tt(yg, yg, ysg, MUL))
                tt(sq2, yg, yg, MUL).then_inc(S["s5_sq"], 1)
                dve.wait_ge(S["conv_rstd"], l + 1)
                dve.wait_ge(S["proj_evac"], EVACS * (l + 1))
                for m in range(2):
                    i = stt(xn[:, 2 + m, :], ucv[:, 6 + m, :], PR(l, "conv_norm")[:, m:m + 1], ucv[:, 1, :], MUL, MUL)
                i.then_inc(S["mix_ready"], 1)
                dve.wait_ge(S["s5_rstd"], l + 1)
                for m in range(2):
                    i = stt(xn[:, m, :], yg[:, m, :], PR(l, "s5_norm")[:, m:m + 1], s5_rstd, MUL, MUL)
                i.then_inc(S["mix_ready"], 1)
                dve.wait_ge(S["mix_ready"], 6 * l + 2)
                V.nop().then_inc(S["s5_mix"], 1)

            def halves(a, m, which):
                return a.rearrange("p (b w m) -> p b w m", w=2, m=m)[:, :, which, :]

            def hgrn(l):
                TINY = 2.0 ** -60
                for hh in range(HEADS):
                    ts(f[:, hh, :], f[:, hh, :], oml[:, hh:hh + 1], lbm[:, hh:hh + 1], MUL, ADD)
                    i = ts(k[:, hh, :], k[:, hh, :], oml[:, hh:hh + 1], None, MUL)
                link(i)
                link(ts(EV[0], f, 1.0 / TINY, 1.0, MUL, ALU.min))
                ts(f, f, TINY, None, ALU.max).then_inc(S["f_in"], 1)
                link(V.memset(R3, 0.0))
                dve.wait_ge(S["f_ln"], l + 1)
                link(tt(EV[0], EV[0], f, ADD))
                for hh in range(HEADS):
                    i = V.tensor_tensor_scan(f[:, hh, :], C("scan"), EV[0][:, hh, :], 0.0, MUL, ADD)
                link(i)
                fb, fk, fq = (a.rearrange("p h t -> p (h t)") for a in (f, k, q))
                n_lv = len(LEVELS)

                def diff(li):
                    m = LEVELS[li]
                    e = EB[li % 2]
                    if li >= 2:
                        dve.wait_ge(S["score"], (n_lv + 1) * HEADS * l + HEADS * (li - 1))
                    ref = halves(fb, m, 0)[:, :, m - 1:m].to_broadcast([P, 2048 // (2 * m), m])
                    tt(halves(e, m, 0), ref, halves(fb, m, 0), SUB)
                    tt(halves(e, m, 1), halves(fb, m, 1), ref, SUB).then_inc(S["b_diff"], 1)

                def use_scores(li):
                    for hh in range(HEADS):
                        dve.wait_ge(S["score"], (n_lv + 1) * HEADS * l + HEADS * li + hh + 1)
                        V.copy_predicated(PT[:, hh, :].rearrange("p (c t) -> p c t", c=NCH),
                                          msk[:, li, :].unsqueeze(1).to_broadcast([P, NCH, P]),
                                          bank[hh + 4 * (li % 2)][:].rearrange("p (c t) -> p c t", c=NCH)
                                          ).then_inc(S["score_used"], 1)

                diff(0)
                for li in range(n_lv):
                    m = LEVELS[li]
                    if li + 1 < n_lv:
                        diff(li + 1)
                    dve.wait_ge(S["b_exp"], n_lv * l + li + 1)
                    e = EB[li % 2]
                    tt(halves(e, m, 0), halves(e, m, 0), halves(fk, m, 0), MUL)
                    tt(halves(e, m, 1), halves(e, m, 1), halves(fq, m, 1), MUL).then_inc(S["b_mul"], 1)
                    if li >= 1:
                        dve.wait_ge(S["score_used"], (n_lv + 1) * HEADS * l + HEADS * (li - 1)) if li > 1 or l else None
                        use_scores(li - 1)
                dve.wait_ge(S["score"], (n_lv + 1) * HEADS * l + HEADS * (n_lv - 1))
                b4 = f.rearrange("p h (c t) -> p (h c) t", c=NCH)
                last = b4[:, :, CH - 1:CH].to_broadcast([P, HEADS * NCH, CH])
                dve.wait_ge(S["score"], (n_lv + 1) * HEADS * l + HEADS * n_lv)
                dve.wait_ge(S["b_mul"], n_lv * (l + 1))
                V.nop().then_inc(S["tail_diff"], 1)
                tt(EB[1].rearrange("p (b t) -> p b t", t=CH), last, b4, SUB).then_inc(S["tail_diff"], 1)
                dve.wait_ge(S["score_used"], (n_lv + 1) * HEADS * l + HEADS * (n_lv - 1))
                use_scores(n_lv - 1)
                dve.wait_ge(S["tail_exp"], 2 * l + 1)
                tt(EB[0], EB[0], fq, MUL).then_inc(S["tail_mul"], 1)
                dve.wait_ge(S["tail_exp"], 2 * l + 2)
                tt(EB[1], EB[1], fk, MUL).then_inc(S["tail_mul"], 1)
                dve.wait_ge(S["score_used"], (n_lv + 1) * HEADS * l + HEADS * n_lv)
                use_scores(n_lv)
                dve.wait_ge(S["s5_mix"], l + 1)
                for c in range(NCH - 1):
                    dve.wait_ge(S["kv"], (NCH - 1) * l + c + 1)
                    if c == 0:
                        V.tensor_copy(St[:, 0, :], bank[4][:]).then_inc(S["states"], 1)
                        continue
                    dve.wait_ge(S["states"], 3 * l + c)
                    link(tt(St[:, c, :].rearrange("p (h d) -> p h d", h=HEADS),
                            St[:, c - 1, :].rearrange("p (h d) -> p h d", h=HEADS),
                            dec[:, :, c:c + 1].to_broadcast([P, HEADS, P]), MUL))
                    tt(St[:, c, :], St[:, c, :], bank[4 + c][:], ADD).then_inc(S["states"], 1)
                for hh in range(HEADS):
                    dve.wait_ge(S["head_rstd"], HEADS * l + hh + 1)
                    link(tt(htmp, bank[hh][:], hrs[:, hh % 2, :], MUL))
                    stt(xn[:, 4 + hh, :], htmp, PR(l, "hg_norm")[:, hh:hh + 1], gate[:, hh, :], MUL, MUL
                        ).then_inc(S["mix_ready"], 1)
                    dve.wait_ge(S["mix_ready"], 6 * l + 3 + hh)

            def add_out(l):
                for m in range(DK):
                    dve.wait_ge(S["wout"], DK * l + m + 1)
                    tt(h[:, m, :], h[:, m, :], bank[m % 2][:], ADD).then_inc(S["y_added"], 1)
                dve.wait_ge(S["y_added"], DK * (l + 1))

            SIL = [0, 1, 0, 1, 0, 1, 2]

            def ffn_products(n, acc, e=None):
                if e is not None:
                    dve.wait_ge(S["sel_w"], e + 1)
                for j in range(GJ):
                    dve.wait_ge(S["silu"], GJ * n + j + 1)
                    dve.wait_ge(S["w13"], 2 * GJ * n + A_SLOTS + 2 * j + 2)
                    tt(g[:, j, :], sil[:, SIL[j], :], bank[2 * SIL[j] + 1][:], MUL).then_inc(S["g_cnt"], 1)
                for m in range(DK):
                    dve.wait_ge(S["y_ready"], DK * n + DK + m + 1)
                    dve.wait_ge(S["y_cnt"], DK * n + 2)
                    tt(acc[:, m, :], acc[:, m, :], bank[6 + m % 2][:], ADD).then_inc(S["y_cnt"], 1)

            def route():
                dve.wait_ge(S["logits"], 1)
                link(V.tensor_copy(lg.rearrange("p i e -> p (i e)"), bank[0][:, 0:4 * E]))
                for i4 in range(4):
                    mine = lg[:, i4, :].unsqueeze(2).to_broadcast([P, E, E])
                    other = lg[:, i4, :].unsqueeze(1).to_broadcast([P, E, E])
                    tt(cmp3[:, i4], other, mine, ALU.is_gt)
                    link(tt(eq3[:, i4], other, mine, ALU.is_equal))
                tri = C("tri8").rearrange("p (e f) -> p e f", e=E)
                for i4 in range(4):
                    i = tt(eq3[:, i4], eq3[:, i4], tri, MUL)
                link(i)
                link(tt(cmp3, cmp3, eq3, ADD))
                link(V.tensor_reduce(rank.rearrange("p i e -> p (i e)"), cmp3.rearrange("p i e f -> p (i e) f"),
                                     AX_X, ADD))
                ts(first, rank, 0.5, None, ALU.is_lt)
                link(ts(selm, rank, 1.5, None, ALU.is_lt))
                link(tt(second, selm, first, SUB))
                V.nop().then_inc(S["route_d"], 1)
                link(tt(rtmp, lg, first, MUL))
                link(V.tensor_reduce(top1, rtmp, AX_X, ADD))
                link(tt(rtmp, lg, second, MUL))
                link(V.tensor_reduce(top2, rtmp, AX_X, ADD))
                tt(dlt, top2, top1, SUB).then_inc(S["route_exp"], 1)
                dve.wait_ge(S["route_exp"], 2)
                link(ts(w1st, w2nd, 1.0, None, ADD))
                link(V.reciprocal(w1st, w1st))
                link(tt(w2nd, w2nd, w1st, MUL))
                bc = lambda a: a.unsqueeze(2).to_broadcast([P, 4, E])
                link(tt(gatem, first, bc(w1st), MUL))
                link(tt(rtmp, second, bc(w2nd), MUL))
                link(tt(gatem, gatem, rtmp, ADD))
                dve.wait_ge(S["posT"], 1)
                link(ts(rtmp.rearrange("p i e -> p (i e)"), bank[1][:, 0:4 * E], 1.0, None, ADD))
                link(tt(rtmp, rtmp, selm, MUL))
                link(ts(posm, rtmp, 1.0, None, SUB))
                link(V.tensor_copy(cnt_i[:], bank[1][:, 4 * E:5 * E]))
                V.nop().then_inc(S["counts_ready"], 1)

            def expert_lists(e, lk):
                for i4 in range(4):
                    ts(posg[:, 0, i4 * P:(i4 + 1) * P], ones, posm[:, i4, bass.ds(e, 1)], None, MUL)
                    i = ts(posg[:, 1, i4 * P:(i4 + 1) * P], ones, gatem[:, i4, bass.ds(e, 1)], None, MUL)
                i.then_inc(S["sel_pos"], 1)
                for i4 in range(4):
                    i = ts(sel[:, i4, :], C("iota"), posm[:, i4, bass.ds(e, 1)], None, ALU.is_equal)
                i.then_inc(S["sel_ready"], 1)
                V.memset(ye, 0.0).then_inc(S["sel_w"], 1)
                dve.wait_ge(S["bc"], e + 1)
                V.tensor_copy(posg[:, 0, :], bank[4][:]).then_inc(S["pos_bc"], 1)
                dve.wait_ge(S["pos_bc"], e + 1)
                for s in range(4):
                    i = stt(G[:, s, :], posg[:, 0, :], C("slot")[:, s:s + 1], bank[5][:], ALU.is_equal, MUL)
                i.then_inc(S["G_ready"], 1)

            dve.wait_ge(S["const_in"], 16)
            V.nop().then_inc(S["g_cnt"], GJ)
            V.nop().then_inc(S["y_cnt"], 2)
            for l in range(DEPTH):
                if l == 0:
                    dve.wait_ge(S["par_in"], 16)
                norm_of_h(2 * l, PR(l, "attn_norm"), xn, "xn_ready")
                dve.wait_ge(S["xn_ready"], DK * (2 * l + 1))
                s5_discretise(l)
                hgrn_bounds(l)
                conv(l)
                s5_rows(l)
                if l == 0:
                    dve.wait_ge(S["glu_in"], 48)
                    link(V.tensor_copy(msk[:], R5[:, 0:(len(LEVELS) + 1) * P].rearrange("p (l t) -> p l t", t=P)))
                s5_scan(l)
                s5_tail(l)
                hgrn(l)
                add_out(l)
                norm_of_h(2 * l + 1, PR(l, "ffn_norm"), xn, "xn_ready")
                if l == 0:
                    with dve.Fori(0, NG) as gi:
                        ffn_products(gi, h)
                    dve.wait_ge(S["y_cnt"], DK * NG + 2)
                else:
                    route()
                    with dve.Fori(0, E) as e:
                        expert_lists(e, link)
                        with dve.Fori(0, NG) as gi:
                            ffn_products(e * NG + gi + NG, ye, e)
                        for m in range(DK):
                            dve.wait_ge(S["scatter"], DK * e + m + 1)
                            tt(h[:, m, :], h[:, m, :], bank[4 + m % 2][:], ADD).then_inc(S["scatter_added"], 1)
                        dve.wait_ge(S["scatter_added"], DK * e + DK)
            norm_of_h(2 * DEPTH, PR(0, "final_norm"), sq, "out_ready")


def _layouts(i):
    import numpy as np
    f = np.float32
    o = {}
    o["x"] = i["x"][0].T.reshape(DK, P, T)
    w = i["w_in"].reshape(DEPTH, DK, P, 24, P)
    order = list(range(0, 8)) + list(range(12, 16)) + list(range(8, 12)) + list(range(16, 24))
    o["win"] = w[:, :, :, order, :].transpose(0, 3, 2, 1, 4).reshape(DEPTH, 12, 2, P, A_W).transpose(0, 1, 3, 2, 4)
    o["win"] = o["win"].reshape(DEPTH, 12, P, B_W)
    w = i["w_out"].reshape(DEPTH, DK, P, 4, 2, P)
    o["wout"] = w.transpose(0, 3, 2, 4, 1, 5).reshape(DEPTH, 4, P, B_W)

    def ffn(w1, w3, w2):
        n = w1.shape[0]
        both = np.stack([w1, w3], 1).reshape(n, 2, DK, P, NG, GJ, P)
        w13 = both.transpose(0, 4, 5, 1, 3, 2, 6).reshape(n * NG, 2 * GJ, P, A_W)
        w2 = w2.reshape(n, NG, GJ, P, B_SLOTS, 2, P).transpose(0, 1, 4, 3, 5, 2, 6).reshape(n * NG, B_SLOTS, P, W2_W)
        return w13, w2
    o["w13a"], o["w2a"] = ffn(i["ffn_w1"], i["ffn_w3"], i["ffn_w2"])
    o["w13e"], o["w2e"] = ffn(i["moe_w1"][0], i["moe_w3"][0], i["moe_w2"][0])

    def tiles(a):
        return a.reshape(-1, P).T

    def states(a):
        a = a.reshape((PAIRS, 2 * S5_N) + a.shape[2:])
        return np.moveaxis(a, 0, 1).reshape(P, -1)
    rows = []
    for l in range(DEPTH):
        c = lambda a: states(a.transpose(0, 2, 1))
        parts = dict(
            attn_norm=tiles(i["attn_norm"][l]), ffn_norm=tiles(i["ffn_norm"][l]), final_norm=tiles(i["final_norm"]),
            lam_re=states(i["s5_lambda_re"][l]), lam_im=states(i["s5_lambda_im"][l]),
            log_dt=states(np.broadcast_to(i["s5_log_dt"][l][:, None], (S5_G, S5_N))),
            b_re=states(i["s5_b_re"][l]), b_im=states(i["s5_b_im"][l]),
            c_re=c(i["s5_c_re"][l]), c_im=c(i["s5_c_im"][l]),
            s5_d=tiles(i["s5_d"][l]), s5_norm=tiles(i["s5_out_norm"][l]),
            conv_w=tiles(i["conv_w"][l]), conv_norm=tiles(i["conv_out_norm"][l]), hg_norm=tiles(i["hg_out_norm"][l]),
            lb0=tiles(i["hg_lower_bounds"][0]), lb1=tiles(i["hg_lower_bounds"][1]))
        rows.append(np.concatenate([parts[n] for n, _ in PARAMS], 1))
    o["par"] = np.stack(rows, 1)
    o["glu"] = i["s5_glu"].reshape(DEPTH, 2, P, 256).transpose(2, 0, 1, 3)
    o["router"] = i["moe_router"][0].reshape(DK, P, E).transpose(1, 0, 2)
    return {k: np.ascontiguousarray(v) for k, v in o.items()}


def _constants():
    import numpy as np
    p = np.arange(P)
    t = np.arange(T)
    e = np.arange(E)
    c = dict(ones=np.ones((P, P)), ident=np.eye(P), before=(p[:, None] < p[None, :]),
             tri8=np.broadcast_to((e[None, :] < e[:, None]).reshape(1, 64), (P, 64)),
             iota=np.broadcast_to(t, (P, T)), scan=np.broadcast_to(t % CH != 0, (P, T)),
             slot=p[:, None] + P * np.arange(4)[None, :], eps=np.full((P, 1), EPS), halfpi=np.full((P, 1), np.pi / 2))
    const = np.concatenate([c[n].astype(np.float32) for n, _ in CONSTS], 1)
    s, q = p[:, None], p[None, :]
    ms = [(s // (2 * m) == q // (2 * m)) & (s % (2 * m) < m) & (q % (2 * m) >= m) for m in LEVELS] + [s == q]
    return np.ascontiguousarray(const), np.ascontiguousarray(np.stack(ms, 1).astype(np.float32))


def kernel(**inputs):
    import numpy as np
    import concourse.bacc as bacc
    from concourse import mybir as mb
    from concourse.bass_utils import run_bass_kernel_spmd

    nc = bacc.Bacc("TRN2", target_bir_lowering=False, num_devices=1)
    arrays = _layouts({k: np.asarray(v) for k, v in inputs.items()})
    arrays["const"], arrays["masks"] = _constants()
    names = ["x", "win", "wout", "w13a", "w2a", "w13e", "w2e", "par", "glu", "router", "const", "masks"]
    args = [nc.dram_tensor("in_" + n, arrays[n].shape, mb.dt.from_np(arrays[n].dtype), kind="ExternalInput").ap()
            for n in names]
    out = nc.dram_tensor("out", (DK, P, T), mb.dt.float32, kind="ExternalOutput").ap()
    build(nc, *args, out)
    r = run_bass_kernel_spmd(nc, [{"in_" + n: arrays[n] for n in names}], core_ids=[0])
    y = r.results[0]["out"]
    return np.ascontiguousarray(y.reshape(D, T).T.reshape(1, T, D))
```

```python
from contextlib import ExitStack

import concourse.bass as bass
from concourse import mybir

P = 128
T = 512
D = 1024
DK = D // P
DEPTH = 2
S5_G, S5_C, S5_N = 16, 16, 64
S5_T = 8
S5_NC = T // S5_T
PAIRS = S5_G // 2
HEADS = 4
CH = 128
NCH = T // CH
LEVELS = [64, 32, 16, 8, 4, 2, 1]
N_SC = (len(LEVELS) + 1) * HEADS
FF = 3584
FT = FF // P
GJ = 4
NG = FT // GJ
E = 8
UW = 8 * P
PROJ, MIX = 24, 32
GU = 3 * GJ
RAW_M, RAW = 6, GU
NH = 3
POOL_UNITS = (2, 6, 10)
DVE_UNITS = tuple(i for i in range(GU) if i not in POOL_UNITS)
NP_, ND_ = len(POOL_UNITS), len(DVE_UNITS)
FFN_UNITS = GU * NG
EPS = 1e-6
WIDTHS = (128, 136, 144, 152, 160, 168, 176, 184, 192, 200, 208, 224, 240, 256, 384, 512)
NARROW = 256

ALU = mybir.AluOpType
ACT = mybir.ActivationFunctionType
AX_X = mybir.AxisListType.X
F32 = mybir.dt.float32
F32R = mybir.dt.float32r
I32 = mybir.dt.int32
U8 = mybir.dt.uint8

PARAMS = [("attn_norm", DK), ("ffn_norm", DK), ("final_norm", DK), ("lam_re", PAIRS), ("lam_im", PAIRS),
          ("log_dt", PAIRS), ("b_re", PAIRS * S5_C), ("b_im", PAIRS * S5_C), ("c_re", PAIRS * S5_C),
          ("c_im", PAIRS * S5_C), ("s5_d", 2), ("s5_norm", 2), ("conv_w", 6), ("conv_norm", 2),
          ("hg_norm", 4), ("lb0", 4), ("lb1", 4)]
PCOL, NPAR = {}, 0
for _n, _w in PARAMS:
    PCOL[_n] = (NPAR, NPAR + _w)
    NPAR += _w

CONSTS = [("ones", P), ("ident", P), ("before", P), ("tri8", 64), ("iota", T), ("slot", 4), ("eps", 1)]
CCOL, NCON = {}, 0
for _n, _w in CONSTS:
    CCOL[_n] = (NCON, NCON + _w)
    NCON += _w

SEMS = """
par_in x_in x_in_late const_in glu_in
hi lo_pool lo_dve used xt xt_hi s5_zero
squares sums rstd_ready xn_ready xn_odd
proj_evac vT vT_evac
s5_dt s5_args s5_sin s5_w s5_wT s5_wT_evac s5_bc s5_k s5_k_evac s5_T_in
s5_us s5_u_out s5_u_in s5_v s5_x s5_y s5_y_evac s5_y_out s5_y_in s5_yd s5_gelu s5_glu s5_sig s5_sq s5_ssq s5_rstd
mix_t mix_h s5_mix conv_sq_in conv_ssq conv_rstd
lb_in lb_exp f_in f_ln b_ready b_diff b_exp b_mul score score_used tail_diff tail_exp tail_mul kdT kdT_evac kv states
head_o head_sq head_ssq head_rstd mix_ready head_low
y_added
silu g_t g_hi g_cnt y_cnt
xtok xtok_evac logits posT route_exp route_d counts_ready sel_pos
sel_ready bc bc_evac G_ready gather gather_evac gates gates_evac gates_kept ye_zero yT yT_hi yT_lo scatter scatter_added
out_ready out_done
act dve
""".split()


def build(nc, x, wmix, wa, we, par, glu, router, const, masks, out):
    u_dram = nc.dram_tensor("u_dram", (DEPTH, 2, P, S5_T, S5_NC), F32, kind="Internal").ap()
    y_dram = nc.dram_tensor("y_dram", (DEPTH, S5_G, S5_C, S5_T, S5_NC), F32, kind="Internal").ap()

    with ExitStack() as ctx:
        def sb(name, shape, dt=F32):
            return ctx.enter_context(nc.sbuf_tensor(name, shape, dt))

        S = {n: ctx.enter_context(nc.semaphore(n)) for n in SEMS}
        raw_full = [ctx.enter_context(nc.semaphore(f"raw_full{i}")) for i in range(RAW)]
        pair = [ctx.enter_context(nc.psum_tensor(f"pair{i}", [P, 2, T], F32)) for i in range(4)]
        bank = [pair[i // 2][:, i % 2, :] for i in range(8)]
        ybank = pair[2:]

        h = sb("h", [P, DK, T])
        x_at = (nc.sbuf_base + 31) // 32 * 32
        xh = sb("xh", [P, DK, T], F32R)
        xe = nc.alloc_sbuf_tensor_at("xe", [P, DK, T], F32, offset=x_at)
        xl = sb("xl", [P, DK, T], F32R)
        w_at = (nc.sbuf_base + 31) // 32 * 32
        wh = sb("wh", [P, NH, UW], F32R)
        wl = sb("wl", [P, NH, UW], F32R)
        sel = nc.alloc_sbuf_tensor_at("sel", [P, 4, T], F32, offset=w_at)
        yl = nc.alloc_sbuf_tensor_at("yl", [P, 4, D], F32R, offset=w_at + 4 * 4 * T)
        place = nc.alloc_sbuf_tensor_at("place", [P, E, T], F32, offset=x_at + 4 * DK * T)
        raw_m = sb("raw_m", [P, RAW_M, UW])
        parm = sb("parm", [P, DEPTH, NPAR])
        con = sb("con", [P, NCON])
        msk = sb("msk", [P, len(LEVELS) + 1, P], U8)
        glu_sb = sb("glu_sb", [P, DEPTH, 2, 256])
        rt_sb = sb("rt_sb", [P, DK, E])
        small = sb("small", [P, 64, PAIRS])
        pw = sb("pw", [P, 2, PAIRS, S5_T + 1])
        bb = sb("bb", [P, 2, PAIRS, S5_C])
        scr_at = (nc.sbuf_base + 31) // 32 * 32
        scr = sb("scr", [P, 24128])

        def over(name, at, shape, dt):
            n = 1
            for k_ in shape[1:]:
                n *= k_
            assert at + n <= 24128
            return nc.alloc_sbuf_tensor_at(name, shape, dt, offset=scr_at + 4 * at)

        def cut(a, n):
            return scr[:, a:a + n]

        C = lambda n: con[:, CCOL[n][0]:CCOL[n][1]]
        PR = lambda l, n: parm[:, l, PCOL[n][0]:PCOL[n][1]]
        ones, ident = C("ones"), C("ident")
        eps = C("eps")
        ucv = cut(0, 4096).rearrange("p (m t) -> p m t", m=8)
        q = cut(4096, 2048).rearrange("p (h t) -> p h t", h=HEADS)
        f = cut(6144, 2048).rearrange("p (h t) -> p h t", h=HEADS)
        k = cut(8192, 2048).rearrange("p (h t) -> p h t", h=HEADS)
        gate = cut(10240, 2048).rearrange("p (h t) -> p h t", h=HEADS)
        v = cut(12288, 2048).rearrange("p (c d) -> p c d", c=NCH)
        EB = [cut(14336, 2048), cut(16384, 2048)]
        R3 = cut(18432, 2048)
        R4 = cut(20480, 2048)
        R5 = scr[:, 22528:24128]
        Tm = R3.rearrange("p (g m) -> p g m", g=S5_G)
        Bst = R4.rearrange("p (q r m) -> p q r m", q=PAIRS, r=2)
        CPn = PAIRS * (S5_T + 1) * S5_C
        cp = [cut(10240 + i * CPn, CPn).rearrange("p (q s c) -> p q s c", q=PAIRS, s=S5_T + 1) for i in range(2)]
        Wst = EB[0].rearrange("p (q r s c) -> p q r s c", q=PAIRS, r=2, s=S5_T)
        Wtmp = EB[1][:, 0:CPn]
        Kst = EB[1].rearrange("p (g m) -> p g m", g=S5_G)
        us = EB[0][:, 0:1024].rearrange("p (j s n) -> p j s n", j=2, s=S5_T)
        U = EB[0][:, 1024:2048].rearrange("p (g n) -> p g n", g=S5_G)
        X = R5[:, 0:1024].rearrange("p (r q n) -> p r q n", r=2, q=PAIRS)
        t1 = EB[1][:, 0:1024].rearrange("p (r q n) -> p r q n", r=2, q=PAIRS)
        t2 = EB[1][:, 1024:2048].rearrange("p (r q n) -> p r q n", r=2, q=PAIRS)
        Ysb = R4[:, 0:1024].rearrange("p (g n) -> p g n", g=S5_G)
        ych = R4[:, 1024:2048].rearrange("p (j s n) -> p j s n", j=2, s=S5_T)
        yg = R4[:, 0:1024].rearrange("p (j t) -> p j t", j=2)
        ysg = R4[:, 1024:2048].rearrange("p (j t) -> p j t", j=2)
        sq2 = R5[:, 0:1024].rearrange("p (j t) -> p j t", j=2)
        s5_rstd = R5[:, 1024:1536]
        sq = scr[:, 4096:4096 + DK * T].rearrange("p (m t) -> p m t", m=DK)
        rstd = scr[:, 8192:8192 + T]
        EV = [e.rearrange("p (h t) -> p h t", h=HEADS) for e in EB]
        PT = R3.rearrange("p (h t) -> p h t", h=HEADS)
        kdT = cut(8192, 2048).rearrange("p (c h d) -> p c h d", c=NCH, h=HEADS)
        ftail = R4.rearrange("p (h t) -> p h t", h=HEADS)
        St = ucv[:, 0:3, :]
        dec = small[:, 60:62, :].rearrange("p a b -> p (a b)").rearrange("p (h c) -> p h c", h=HEADS)
        hsq, hrs, htmp = EV[1], EV[0], PT
        gh = over("gh", 0, [P, GJ, T], F32R)
        gl = over("gl", GJ * T, [P, GJ, T], F32R)
        g = cut(0, GJ * T).rearrange("p (j t) -> p j t", j=GJ)
        sil = cut(4096, 1024).rearrange("p (j t) -> p j t", j=2)
        gt = cut(5120, 1024).rearrange("p (j t) -> p j t", j=2)
        yh = over("yh", 0, [P, 4, D], F32R)
        ye = cut(6144, 4096).rearrange("p (m t) -> p m t", m=DK)
        xtok = cut(10240, 4096).rearrange("p (i d) -> p i d", i=4)
        G = over("G", 14336, [P, 4, T], F32R)
        posg = cut(16384, 1024).rearrange("p (r t) -> p r t", r=2)
        RAW_X = 17408
        rsm = cut(6144, 2048)
        rv = lambda i, n=32: rsm[:, i * 64:i * 64 + n]
        lg = rv(0).rearrange("p (i e) -> p i e", i=4)
        cmp3 = rsm[:, 1024:1280].rearrange("p (i e f) -> p i e f", i=4, e=E)
        eq3 = rsm[:, 1280:1536].rearrange("p (i e f) -> p i e f", i=4, e=E)
        rank, selm, first, second = (rv(i).rearrange("p (i e) -> p i e", i=4) for i in (1, 2, 3, 4))
        top1, top2 = rv(5, 4), rv(6, 4)
        dlt, w2nd, w1st = rv(7, 4), rv(8, 4), rv(9, 4)
        flat_small = small[:].rearrange("p a b -> p (a b)")
        gate9, pos9 = (flat_small[:, i * 36:i * 36 + 36].rearrange("p (i e) -> p i e", i=4) for i in range(2))
        gatem, posm = gate9[:, :, 0:E], pos9[:, :, 0:E]
        rtmp = rv(12).rearrange("p (i e) -> p i e", i=4)
        cnt_i = sb("cnt_i", [P, E + 1], I32)
        gslot = sb("gslot", [P, 2, 4])
        omx = small[:, 48:52, :].rearrange("p a b -> p (a b)")
        lbm, oml = small[:, 52, 0:4], small[:, 53, 0:4]
        xt = cut(8704, 2048).rearrange("p (m t) -> p m t", m=4)
        iT = ucv[:, 2:6, :]

        def raw(i):
            return raw_m[:, i, :] if i < RAW_M else scr[:, RAW_X + (i - RAW_M) * UW:RAW_X + (i - RAW_M + 1) * UW]

        def sum_bank(n):
            return bank[2][:] if n == 2 else bank[6]

        def units_before(l):
            return (MIX + FFN_UNITS) * l

        def pool_before(l):
            return (MIX + NP_ * NG) * l

        def group_unit(l, n, i):
            return MIX * (l + 1) + GU * n + i + 1

        def loads(l, s):
            return (l + 1) * len(range(s, MIX, RAW_M)) if s < RAW_M else 0

        def lo_ready(eng, l, n, i):
            if i in POOL_UNITS:
                eng.wait_ge(S["lo_pool"], MIX * (l + 1) + NP_ * n + POOL_UNITS.index(i) + 1)
            else:
                eng.wait_ge(S["lo_dve"], ND_ * (n + 1) + DVE_UNITS.index(i) + 1)

        def chain(eng, s):
            n = [0]

            def link(ins):
                n[0] += 1
                ins.then_inc(s, 1)
                eng.wait_ge(s, n[0])
            link.count = n
            return link

        block = ctx.enter_context(nc.Block())

        @block.sync
        def _(sp):
            for kk in range(DK):
                sp.dma_start(h[:, kk, :], x[kk]).then_inc(S["x_in" if kk < DK // 2 else "x_in_late"], 16)
            sp.dma_start(con[:], const).then_inc(S["const_in"], 16)
            sp.dma_start(parm[:], par).then_inc(S["par_in"], 16)

            def load(s, src):
                sp.dma_start(raw(s), src).then_inc(raw_full[s], 16)

            def group(l, src, gi, n, units=GU):
                for i in range(units):
                    if i == RAW_M:
                        sp.wait_ge(S["used"], units_before(l) + PROJ + 1)
                    if l == 0:
                        lo_ready(sp, l, n - 1, i)
                    else:
                        sp.wait_ge(S["used"], group_unit(l, n - 1, i))
                    load(i, src[bass.ds(gi, 1), i].rearrange("a p c -> (a p) c"))

            for l in range(DEPTH):
                for u in range(MIX):
                    if u >= RAW_M:
                        sp.wait_ge(S["lo_pool"], pool_before(l) + u - RAW_M + 1)
                    elif l > 0 and u == 0:
                        sp.wait_ge(S["lo_pool"], pool_before(l))
                        sp.wait_ge(S["lo_dve"], ND_ * (NG + 1))
                    load(u % RAW_M, wmix[l, u])
                    if l == 0 and u == RAW_M - 1:
                        sp.dma_start(R5[:, 0:(len(LEVELS) + 1) * P].rearrange("p (l t) -> p l t", t=P), masks
                                     ).then_inc(S["glu_in"], 16)
                        sp.dma_start(glu_sb[:], glu).then_inc(S["glu_in"], 16)
                        sp.dma_start(rt_sb[:], router).then_inc(S["glu_in"], 16)
                    if u == 12:
                        sp.wait_ge(S["s5_us"], l + 1)
                        sp.dma_start(u_dram[l].rearrange("j p s n -> p j s n"), us).then_inc(S["s5_u_out"], 16)
                        sp.wait_ge(S["s5_u_out"], 16 * (l + 1))
                        for r in range(S5_T):
                            sp.dma_start(U[r * S5_C:(r + 1) * S5_C, :, :],
                                         u_dram[l, :, :, S5_T - 1 - r, :].rearrange("j (g c) n -> c (j g) n", c=S5_C)
                                         ).then_inc(S["s5_u_in"], 16)
                        sp.wait_ge(S["s5_zero"], l + 1)
                        sp.wait_ge(S["s5_k_evac"], 4 * (l + 1))
                        for r in range(S5_T):
                            sp.dma_start(Tm[r * S5_C:(r + 1) * S5_C, :, (S5_T - 1 - r) * S5_C:P],
                                         Kst[0:S5_C, :, 0:(r + 1) * S5_C]).then_inc(S["s5_T_in"], 16)
                    if u == 22:
                        sp.wait_ge(S["s5_y_evac"], 2 * (l + 1))
                        for t in range(S5_T):
                            for w in range(2):
                                sp.dma_start(
                                    y_dram[l, :, :, t, :].rearrange("(q w) c n -> w c q n", w=2)[w],
                                    Ysb[t * S5_C:(t + 1) * S5_C, w * PAIRS:(w + 1) * PAIRS, :]
                                    ).then_inc(S["s5_y_out"], 16)
                        sp.wait_ge(S["s5_y_out"], 2 * 16 * S5_T * (l + 1))
                        sp.dma_start(ych, y_dram[l].rearrange("(j g) c s n -> (g c) j s n", j=2)
                                     ).then_inc(S["s5_y_in"], 16)
                sp.wait_ge(S["lo_pool"], pool_before(l) + MIX)
                if l == 0:
                    with sp.Fori(0, NG) as gi:
                        group(l, wa, gi, gi)
                else:
                    with sp.Fori(0, E * NG) as gi:
                        group(l, we, gi, gi + NG)
            for m in range(DK):
                sp.wait_ge(S["out_ready"], m + 1)
                sp.dma_start(out[m], sq[:, m, :]).then_inc(S["out_done"], 16)
            sp.wait_ge(S["out_done"], 16 * DK)

        @block.gpsimd
        def _(pool):
            def low(s, hs, count):
                pool.wait_ge(S["hi"], count)
                nc.gpsimd.tensor_tensor(wl[:, hs, :], raw(s), wh[:, hs, :].bitcast(F32), ALU.subtract
                                        ).then_inc(S["lo_pool"], 1)

            def low_odd(n):
                for kk in range(1, DK, 2):
                    pool.wait_ge(S["xt_hi"], DK * n + kk + 1)
                    nc.gpsimd.tensor_tensor(xl[:, kk, :], xt[:, kk % 4, :], xh[:, kk, :].bitcast(F32), ALU.subtract
                                            ).then_inc(S["xn_odd"], 1)

            for l in range(DEPTH):
                for u in range(MIX):
                    if u == NH:
                        low_odd(2 * l)
                    if u == PROJ + NH:
                        for hh in range(HEADS):
                            pool.wait_ge(S["mix_h"], DK * l + 4 + hh + 1)
                            nc.gpsimd.tensor_tensor(xl[:, 4 + hh, :], q[:, hh, :], xh[:, 4 + hh, :].bitcast(F32),
                                                    ALU.subtract).then_inc(S["head_low"], 1)
                    low(u % RAW_M, u % NH, units_before(l) + u + 1)
                if l == 0:
                    low_odd(1)
                    with pool.Fori(0, NG) as gi:
                        for i in POOL_UNITS:
                            low(i, i % NH, group_unit(l, gi, i))

        @block.tensor
        def _(pe):
            mm = nc.tensor.matmul

            def norm_sums(n):
                for kk in range(DK):
                    pe.wait_ge(S["squares"], DK * n + kk + 1)
                    i = mm(sum_bank(n), ones, sq[:, kk, :], start=(kk == 0), stop=(kk == DK - 1))
                i.then_inc(S["sums"], 1)

            def normed(n, kk):
                pe.wait_ge(S["xn_odd" if kk % 2 else "xn_ready"], 4 * n + kk // 2 + 1)

            def product(o, hs, tiles, lo_wait, tile_wait=None):
                for n, (rh, rl) in enumerate(tiles):
                    if tile_wait:
                        tile_wait(n)
                    w_ = wh[:, hs, n * P:(n + 1) * P]
                    mm(o, w_, rh, start=(n == 0), stop=False)
                    mm(o, w_, rl, start=False, stop=False)
                lo_wait()
                for n, (rh, rl) in enumerate(tiles):
                    i = mm(o, wl[:, hs, n * P:(n + 1) * P], rh, start=False, stop=(n == len(tiles) - 1))
                i.then_inc(S["used"], 1)

            def mixer_unit(l, u, o, tile_wait=None):
                pe.wait_ge(S["hi"], units_before(l) + u + 1)
                product(o, u % NH, [(xh[:, kk, :], xl[:, kk, :]) for kk in range(DK)],
                        lambda: pe.wait_ge(S["lo_pool"], pool_before(l) + u + 1), tile_wait)

            def projection(l, units):
                for u in units:
                    if PROJ * l + u >= 4:
                        pe.wait_ge(S["proj_evac"], PROJ * l + u - 3)
                    mixer_unit(l, u, bank[u % 4][:],
                               (lambda kk: normed(2 * l, kk)) if u == 0 else None)

            def value_rows(l):
                pe.wait_ge(S["proj_evac"], PROJ * (l + 1))
                for c in range(NCH):
                    if c >= 2:
                        pe.wait_ge(S["vT_evac"], NCH * l + c - 1)
                    for m in range(4):
                        i = nc.tensor.transpose(bank[2 + c % 2][:, m * P:(m + 1) * P], iT[:, m, c * CH:(c + 1) * CH],
                                                ident)
                    i.then_inc(S["vT"], 1)

            def s5_matrices(l):
                pe.wait_ge(S["s5_w"], l + 1)
                for pr in range(PAIRS):
                    for r in range(2):
                        n = 2 * pr + r
                        i = nc.tensor.transpose(bank[4 + n // 4][:, (n % 4) * P:(n % 4 + 1) * P],
                                                Wst[:, pr, r].rearrange("p s c -> p (s c)"), ident)
                        if n % 4 == 3:
                            i.then_inc(S["s5_wT"], 1)
                pe.wait_ge(S["s5_bc"], l + 1)
                for gg in range(S5_G):
                    a, pr = 64 * (gg // PAIRS), gg % PAIRS
                    if gg % 4 == 0:
                        pe.wait_ge(S["s5_wT_evac"], 4 * l + gg // 4 + 1)
                    o = bank[4 + gg // 4][0:S5_C, (gg % 4) * P:(gg % 4 + 1) * P]
                    for r in range(2):
                        i = mm(o, bb[a:a + 64, r, pr, :], cp[r][a:a + 64, pr, 0:S5_T, :].rearrange("p s c -> p (s c)"),
                               start=(r == 0), stop=(r == 1))
                    if gg % 4 == 3:
                        i.then_inc(S["s5_k"], 1)

            def s5_in(l):
                pe.wait_ge(S["s5_k_evac"], 4 * (l + 1))
                pe.wait_ge(S["s5_u_in"], 16 * S5_T * (l + 1))
                for r in range(2):
                    for gg in range(S5_G):
                        a, pr = 64 * (gg % 2), gg // 2
                        i = mm(bank[4 + r][a:a + 64, pr * S5_NC:(pr + 1) * S5_NC], Bst[:, pr, r, a:a + 64],
                               U[:, gg, :], start=True, stop=True)
                i.then_inc(S["s5_v"], 1)

            def s5_out(l):
                pe.wait_ge(S["s5_T_in"], 16 * S5_T * (l + 1))
                pe.wait_ge(S["s5_x"], l + 1)
                for gg in range(S5_G):
                    a, pr = 64 * (gg // PAIRS), gg % PAIRS
                    o = bank[6 + gg // PAIRS]
                    c0 = pr * S5_NC
                    mm(o[:, c0:c0 + S5_NC], Tm[:, gg, :], U[:, 2 * pr + gg // PAIRS, :], start=True, stop=False)
                    for r in range(2):
                        i = mm(o[:, c0 + 1:c0 + S5_NC],
                               cp[r][a:a + 64, pr, 1:S5_T + 1, :].rearrange("p s c -> p (s c)"),
                               X[a:a + 64, r, pr, 0:S5_NC - 1], start=False, stop=(r == 1))
                    if gg % 8 == 7:
                        i.then_inc(S["s5_y"], 1)

            def s5_glu(l):
                pe.wait_ge(S["s5_gelu"], l + 1)
                for m in range(2):
                    for kk in range(2):
                        i = mm(bank[m][:], glu_sb[:, l, kk, m * P:(m + 1) * P], yg[:, kk, :],
                               start=(kk == 0), stop=(kk == 1))
                i.then_inc(S["s5_glu"], 1)

            def s5_norm(l):
                pe.wait_ge(S["s5_sq"], l + 1)
                for m in range(2):
                    i = mm(bank[3][:], ones, sq2[:, m, :], start=(m == 0), stop=(m == 1))
                i.then_inc(S["s5_ssq"], 1)

            def conv_norm(l):
                pe.wait_ge(S["conv_sq_in"], l + 1)
                for m in range(2):
                    i = mm(bank[7], ones, ucv[:, 4 + m, :], start=(m == 0), stop=(m == 1))
                i.then_inc(S["conv_ssq"], 1)

            def scores(l, s):
                if s == 0:
                    pe.wait_ge(S["s5_y_evac"], 2 * (l + 1))
                    pe.wait_ge(S["f_in"], l + 1)
                    pe.wait_ge(S["proj_evac"], PROJ * l + 16)
                else:
                    pe.wait_ge(S["b_mul"], len(LEVELS) * l + s)
                for hh in range(HEADS):
                    if s > 0:
                        pe.wait_ge(S["score_used"], N_SC * l + HEADS * (s - 1) + hh + 1)
                    for c in range(NCH):
                        cols = slice(c * CH, (c + 1) * CH)
                        lhs = EV[(s - 1) % 2][:, hh, cols] if s else k[:, hh, cols]
                        rhs = lhs if s else q[:, hh, cols]
                        i = mm(bank[hh + 4][:, cols], lhs, rhs, start=True, stop=True)
                    i.then_inc(S["score"], 1)

            def hgrn(l):
                pe.wait_ge(S["tail_mul"], 2 * l + 1)
                pe.wait_ge(S["score_used"], N_SC * (l + 1))
                for c in range(NCH):
                    for hh in range(HEADS):
                        i = nc.tensor.transpose(bank[4 + c][:, hh * P:(hh + 1) * P], EV[1][:, hh, c * CH:(c + 1) * CH],
                                                ident)
                    i.then_inc(S["kdT"], 1)
                pe.wait_ge(S["vT_evac"], NCH * (l + 1))
                for c in range(NCH - 1):
                    pe.wait_ge(S["kdT_evac"], NCH * l + c + 1)
                    for hh in range(HEADS):
                        i = mm(bank[4 + c][:, hh * P:(hh + 1) * P], kdT[:, c, hh, :], v[:, c, hh * P:(hh + 1) * P],
                               start=True, stop=True)
                    i.then_inc(S["kv"], 1)
                s5_norm(l)
                pe.wait_ge(S["tail_mul"], 2 * l + 2)
                for hh in range(HEADS):
                    if hh == 3:
                        pe.wait_ge(S["s5_rstd"], l + 1)
                    for c in range(NCH):
                        if c > 0 and hh == 0:
                            pe.wait_ge(S["states"], 3 * l + c)
                        o = bank[hh][:, c * CH:(c + 1) * CH]
                        i = mm(o, v[:, c, hh * P:(hh + 1) * P], PT[:, hh, c * CH:(c + 1) * CH],
                               start=True, stop=(c == 0))
                        if c > 0:
                            i = mm(o, St[:, c - 1, hh * P:(hh + 1) * P], EV[0][:, hh, c * CH:(c + 1) * CH],
                                   start=False, stop=True)
                    i.then_inc(S["head_o"], 1)
                pe.wait_ge(S["kdT_evac"], NCH * (l + 1))
                for hh in range(HEADS):
                    pe.wait_ge(S["head_sq"], HEADS * l + hh + 1)
                    mm(bank[4 + hh], ones, hsq[:, hh, :], start=True, stop=True).then_inc(S["head_ssq"], 1)

            def out_projection(l):
                for m in range(DK):
                    if m >= 2:
                        pe.wait_ge(S["y_added"], DK * l + m - 1)
                    if m == 0:
                        pe.wait_ge(S["head_rstd"], HEADS * l + 1)
                    mixer_unit(l, PROJ + m, bank[4 + m % 2],
                               (lambda kk: pe.wait_ge(S["mix_ready"], 4 * (l + 1)) if kk < 4 else
                                pe.wait_ge(S["head_low"], HEADS * l + kk - 3)) if m == 0 else None)

            def expert_group(n, W, e):
                for j in range(GJ):
                    pe.wait_ge(S["g_cnt"], GJ * n + j - 1)
                    if j < 2:
                        pe.wait_ge(S["scatter_added"], DK // 2 * e + j + 1)
                    for w in range(2):
                        i_ = 2 * j + w
                        pe.wait_ge(raw_full[i_], 16 * (loads(1, i_) + n + 1))
                        for kk in range(DK):
                            i = mm(bank[2 * (j % 2) + w][:, 0:W], raw(i_)[:, kk * P:(kk + 1) * P], xe[:, kk, 0:W],
                                   start=(kk == 0), stop=(kk == DK - 1))
                        i.then_inc(S["used"], 1)

                def share(q_, js):
                    for m in range(2):
                        for j in js:
                            i = mm(ybank[q_ % 2][:, m, 0:W], raw(2 * GJ + q_)[:, (m * GJ + j) * P:(m * GJ + j + 1) * P],
                                   g[:, j, 0:W], start=(j == 0), stop=(j == GJ - 1))
                    return i

                pe.wait_ge(S["g_cnt"], GJ * n + GJ - 1)
                for q_, js in ((0, range(GJ - 1)), (1, (0,))):
                    pe.wait_ge(S["y_cnt"], 4 * n + q_ + 1)
                    pe.wait_ge(raw_full[2 * GJ + q_], 16 * (loads(1, 2 * GJ + q_) + n + 1))
                    share(q_, js)
                pe.wait_ge(S["g_cnt"], GJ * n + GJ)
                share(0, (GJ - 1,)).then_inc(S["used"], 1)
                share(1, range(1, GJ)).then_inc(S["used"], 1)
                for q_ in range(2, 4):
                    pe.wait_ge(S["y_cnt"], 4 * n + q_ + 1)
                    pe.wait_ge(raw_full[2 * GJ + q_], 16 * (loads(1, 2 * GJ + q_) + n + 1))
                    share(q_, range(GJ)).then_inc(S["used"], 1)

            def ffn_group(l, n, W):
                for j in range(GJ):
                    pe.wait_ge(S["g_t"], GJ * n + j + 1)
                    for w in range(2):
                        i_ = 2 * j + w
                        pe.wait_ge(S["hi"], group_unit(l, n, i_))
                        product(bank[2 * (j % 2) + w][:, 0:W], i_ % NH,
                                [(xh[:, kk, 0:W], xl[:, kk, 0:W]) for kk in range(DK)],
                                lambda: lo_ready(pe, l, n, i_),
                                (lambda kk: normed(2 * l + 1, kk))
                                if i_ == 0 else None)
                for q_ in range(4):
                    i_ = 2 * GJ + q_
                    hs = i_ % NH
                    pe.wait_ge(S["y_cnt"], 4 * n + q_ + 1)
                    pe.wait_ge(S["hi"], group_unit(l, n, i_))
                    blk = lambda w_, m, j: w_[:, hs, (m * GJ + j) * P:(m * GJ + j + 1) * P]
                    for js in (range(GJ - 1), (GJ - 1,)):
                        for m in range(2):
                            o = ybank[q_ % 2][:, m, 0:W]
                            for j in js:
                                if q_ == 0 and m == 0:
                                    pe.wait_ge(S["g_cnt"], GJ * n + j + 1)
                                mm(o, blk(wh, m, j), gh[:, j, 0:W], start=(j == 0), stop=False)
                                mm(o, blk(wh, m, j), gl[:, j, 0:W], start=False, stop=False)
                    lo_ready(pe, l, n, i_)
                    for m in range(2):
                        for j in range(GJ):
                            i = mm(ybank[q_ % 2][:, m, 0:W], blk(wl, m, j), gh[:, j, 0:W], start=False,
                                   stop=(j == GJ - 1))
                    i.then_inc(S["used"], 1)

            def route():
                for i4 in range(4):
                    for kk in range(DK):
                        i = mm(bank[0][:, i4 * E:(i4 + 1) * E], xe[:, kk, i4 * P:(i4 + 1) * P], rt_sb[:, kk, :],
                               start=(kk == 0), stop=(kk == DK - 1))
                i.then_inc(S["logits"], 1)
                for i4 in range(4):
                    for half in range(2):
                        n = 2 * i4 + half
                        if n >= 4:
                            pe.wait_ge(S["xtok_evac"], n - 3)
                        for c in range(4):
                            i = nc.tensor.transpose(bank[4 + n % 4][:, c * P:(c + 1) * P],
                                                    xe[:, 4 * half + c, i4 * P:(i4 + 1) * P], ident)
                        i.then_inc(S["xtok"], 1)
                pe.wait_ge(S["route_d"], 1)
                for i4 in range(4):
                    for j4 in range(i4 + 1):
                        mm(bank[1][:, i4 * E:(i4 + 1) * E], C("before") if j4 == i4 else ones, selm[:, j4, :],
                           start=(j4 == 0), stop=(j4 == i4))
                for j4 in range(4):
                    i = mm(bank[1][:, 4 * E:5 * E], ones, selm[:, j4, :], start=(j4 == 0), stop=(j4 == 3))
                i.then_inc(S["posT"], 1)

            def spread(e):
                pe.wait_ge(S["sel_pos"], e + 1)
                if e >= 2:
                    pe.wait_ge(S["bc_evac"], e - 1)
                for i4 in range(4):
                    i = mm(bank[4 + e % 2][:, i4 * P:(i4 + 1) * P], posg[:, e % 2, i4 * P:(i4 + 1) * P], ident,
                           start=True, stop=True)
                i.then_inc(S["bc"], 1)

            def gather(e, W):
                pe.wait_ge(S["g_cnt"], GJ * NG * (e + 1))
                pe.wait_ge(S["sel_ready"], e + 1)
                for m in range(DK):
                    if m >= 4:
                        pe.wait_ge(S["gather_evac"], DK * e + m - 3)
                    for i4 in range(4):
                        i = mm(bank[m % 4][:, 0:W], xtok[:, i4, m * P:(m + 1) * P], sel[:, i4, 0:W],
                               start=(i4 == 0), stop=(i4 == 3))
                    i.then_inc(S["gather"], 1)
                pe.wait_ge(S["gather_evac"], DK * e + 5)
                for s in range((W + P - 1) // P):
                    for i4 in range(4):
                        i = mm(bank[0][:, s:s + 1], sel[:, i4, s * P:(s + 1) * P], gate9[:, i4, bass.ds(e, 1)],
                               start=(i4 == 0), stop=(i4 == 3))
                i.then_inc(S["gates"], 1)

            def groups(e, W):
                with pe.Fori(0, NG // 2) as gi:
                    for half in range(2):
                        expert_group(e * NG + gi * 2 + NG + half, W, e)
                expert_group(e * NG + 2 * NG - 1, W, e)

            def rows(e, tiles):
                pe.wait_ge(S["y_cnt"], 4 * NG * e + 4 * 2 * NG + 2)
                for s in range(tiles):
                    for half in range(2):
                        n = 2 * s + half
                        if n >= 4:
                            pe.wait_ge(S["yT_lo"], 8 * e + n - 3)
                        for c in range(4):
                            i = nc.tensor.transpose(bank[4 + n % 4][:, c * P:(c + 1) * P],
                                                    ye[:, 4 * half + c, s * P:(s + 1) * P], ident)
                        i.then_inc(S["yT"], 9 - 2 * tiles if n == 2 * tiles - 1 else 1)

            def scatter(e, tiles):
                pe.wait_ge(S["G_ready"], e + 1)
                pe.wait_ge(S["gates_evac"], e + 2)
                for m2 in range(DK // 2):
                    pe.wait_ge(S["yT_lo"], 8 * e + (2 * tiles - 1 if m2 < 2 else 8))
                    for m in (2 * m2, 2 * m2 + 1):
                        for s in range(tiles):
                            for part in (yh, yl):
                                i = mm(bank[m], part[:, s, m * P:(m + 1) * P], G[:, s, :],
                                       start=(s == 0 and part is yh), stop=(s == tiles - 1 and part is yl))
                    i.then_inc(S["scatter"], 1)

            def by_count(n, ws, body):
                if len(ws) == 1:
                    body(ws[0])
                    return
                half = len(ws) // 2
                with pe.If(n <= ws[half - 1]):
                    by_count(n, ws[:half], body)
                    pe.nop()
                with pe.Else():
                    by_count(n, ws[half:], body)
                    pe.nop()

            def count_of(e):
                return pe.value_load(cnt_i[0:1, bass.ds(e, 1)], min_val=-1, max_val=T)

            pe.wait_ge(S["const_in"], 16)
            for l in range(DEPTH):
                norm_sums(2 * l)
                projection(l, range(0, 8))
                s5_matrices(l)
                projection(l, range(8, 10))
                s5_in(l)
                projection(l, range(10, 12))
                conv_norm(l)
                projection(l, range(12, 18))
                s5_out(l)
                for s in range(8):
                    if 0 < s < 7:
                        projection(l, range(17 + s, 18 + s))
                    elif s == 7:
                        value_rows(l)
                    scores(l, s)
                if l == 0:
                    pe.wait_ge(S["glu_in"], 48)
                s5_glu(l)
                hgrn(l)
                out_projection(l)
                norm_sums(2 * l + 1)
                if l == 0:
                    with pe.Fori(0, NG) as gi:
                        ffn_group(0, gi, T)
                else:
                    pe.wait_ge(S["xn_ready"], 4 * 3 + DK)
                    route()
                    pe.wait_ge(S["xtok_evac"], 8)
                    pe.wait_ge(S["counts_ready"], 1)
                    for e in range(E):
                        spread(e)
                    pe.wait_ge(S["bc_evac"], E)
                    pe.wait_ge(S["sel_ready"], 1)
                    by_count(count_of(0), list(WIDTHS), lambda W: gather(0, W))
                    pe.wait_ge(S["gates_evac"], 1)
                    with pe.Fori(0, E) as e:
                        n_tok = count_of(e)
                        by_count(n_tok, list(WIDTHS), lambda W: groups(e, W))
                        n_next = count_of(e + 1)
                        by_count(n_tok, [P, 2 * P, T], lambda W: rows(e, W // P))
                        with pe.If(n_next >= 0):
                            by_count(n_next, list(WIDTHS), lambda W: gather(e + 1, W))
                            pe.nop()
                        by_count(n_tok, [P, 2 * P, T], lambda W: scatter(e, W // P))
                    pe.wait_ge(S["scatter_added"], DK // 2 * (E + 1))
                    norm_sums(2 * DEPTH)

        @block.scalar
        def _(act):
            fn = nc.scalar.activation
            link = chain(act, S["act"])

            def norm_rstd(s_wait, n, ps, dst, width, s_done):
                act.wait_ge(S[s_wait], n)
                link(fn(dst, ps, ACT.Ln, bias=eps, scale=1.0 / width))
                fn(dst, dst, ACT.Exp, scale=-0.5).then_inc(S[s_done], 1)

            def high(full, s, hs):
                act.wait_ge(raw_full[s], 16 * full)
                fn(wh[:, hs, :], raw(s), ACT.Copy).then_inc(S["hi"], 1)

            def mixer_high(l, u):
                if u >= MIX:
                    return
                s = u % RAW_M
                full = (loads(l - 1, s) + NG if l else 0) + u // RAW_M + 1
                if units_before(l) + u >= NH:
                    act.wait_ge(S["used"], units_before(l) + u + 1 - NH)
                high(full, s, u % NH)

            def group_high(l, n, i):
                if i >= GU:
                    n, i = n + 1, i - GU
                high(loads(l, i) + n + 1, i, i % NH)

            def evac(l, idx, dst, func=ACT.Copy, inc=True, scale=1.0):
                act.wait_ge(S["used"], units_before(l) + idx + 1)
                i = fn(dst, bank[idx % 4][:], func, scale=scale)
                if inc:
                    i.then_inc(S["proj_evac"], 1)
                    mixer_high(l, idx + NH)

            def mix_high(l, n, tile, src):
                act.wait_ge(S["mix_t"], DK * l + n + 1)
                fn(xh[:, tile, :], src, ACT.Copy).then_inc(S["mix_h"], 1)

            def mixers(l):
                if l > 0:
                    act.wait_ge(S["s5_mix"], l)
                act.wait_ge(S["par_in"], 16)
                fn(small[:, 0, :], PR(l, "log_dt"), ACT.Exp).then_inc(S["s5_dt"], 1)
                for i in range(3):
                    evac(l, i, ucv[:, i, :])
                act.wait_ge(S["s5_args"], l + 1)
                fn(small[:, 3, :], small[:, 1, :], ACT.Exp)
                fn(small[:, 5, :], small[:, 4, :], ACT.Sin)
                fn(small[:, 7, :], small[:, 6, :], ACT.Sin).then_inc(S["s5_sin"], 1)
                act.wait_ge(S["lb_in"], l + 1)
                fn(omx[:, 8:16], omx[:, 0:8], ACT.Exp).then_inc(S["lb_exp"], 1)
                for i in range(3, 8):
                    evac(l, i, ucv[:, i, :])
                for i in range(4):
                    act.wait_ge(S["s5_wT"], 4 * l + i + 1)
                    fn(R4[:, i * T:(i + 1) * T], bank[4 + i], ACT.Copy).then_inc(S["s5_wT_evac"], 1)
                for i in range(4):
                    act.wait_ge(S["s5_k"], 4 * l + i + 1)
                    if i == 0:
                        act.wait_ge(S["s5_bc"], l + 1)
                    fn(Kst[0:S5_C].rearrange("p g m -> p (g m)")[:, i * T:(i + 1) * T], bank[4 + i][0:S5_C, :],
                       ACT.Copy).then_inc(S["s5_k_evac"], 1)
                for i in range(4):
                    evac(l, 8 + i, f[:, i, :], ACT.Sigmoid, inc=False)
                    evac(l, 8 + i, k[:, i, :], ACT.Sigmoid, scale=-1.0)
                norm_rstd("conv_ssq", l + 1, bank[7], s5_rstd, 256, "conv_rstd")
                for i in range(2):
                    evac(l, 12 + i, q[:, i, :], ACT.Silu)
                act.wait_ge(S["f_in"], l + 1)
                fn(f, f, ACT.Ln)
                fn(ftail, ftail, ACT.Ln).then_inc(S["f_ln"], 1)
                for i in range(2, 4):
                    evac(l, 12 + i, q[:, i, :], ACT.Silu)
                for i in range(2):
                    evac(l, 16 + i, iT[:, i, :])
                act.wait_ge(S["b_ready"], l + 1)
                for i in range(2):
                    act.wait_ge(S["s5_y"], 2 * l + i + 1)
                    fn(Ysb[:, 8 * i:8 * i + 8, :].rearrange("p g n -> p (g n)"), bank[6 + i],
                       ACT.Copy).then_inc(S["s5_y_evac"], 1)
                for li in range(len(LEVELS)):
                    act.wait_ge(S["b_diff"], len(LEVELS) * l + li + 1)
                    fn(EB[li % 2], EB[li % 2], ACT.Exp).then_inc(S["b_exp"], 1)
                    idx = 18 + li
                    if idx < PROJ:
                        evac(l, idx, iT[:, idx - 16, :] if idx < 20 else gate[:, idx - 20, :])
                    if li == 4:
                        act.wait_ge(S["s5_yd"], l + 1)
                        fn(yg, yg, ACT.Gelu_apprx_tanh).then_inc(S["s5_gelu"], 1)
                for c in range(NCH):
                    act.wait_ge(S["vT"], NCH * l + c + 1)
                    fn(v[:, c, :], bank[2 + c % 2][:], ACT.Copy).then_inc(S["vT_evac"], 1)
                act.wait_ge(S["tail_diff"], l + 1)
                fn(EB[1], EB[1], ACT.Exp).then_inc(S["tail_exp"], 1)
                act.wait_ge(S["score"], N_SC * (l + 1))
                fn(dec, f.rearrange("p h (c t) -> p h c t", c=NCH)[:, :, :, CH - 1], ACT.Exp)
                fn(EV[0], f, ACT.Exp).then_inc(S["tail_exp"], 1)
                act.wait_ge(S["s5_glu"], l + 1)
                for m in range(2):
                    i = fn(ysg[:, m, :], bank[m][:], ACT.Sigmoid)
                i.then_inc(S["s5_sig"], 1)
                for c in range(NCH):
                    act.wait_ge(S["kdT"], NCH * l + c + 1)
                    fn(kdT[:, c].rearrange("p h d -> p (h d)"), bank[4 + c], ACT.Copy).then_inc(S["kdT_evac"], 1)
                for m in range(2):
                    mix_high(l, m, 2 + m, ucv[:, 6 + m, :])
                norm_rstd("s5_ssq", l + 1, bank[3][:], s5_rstd, 256, "s5_rstd")
                fn(gate, gate, ACT.Silu)
                for m in range(2):
                    mix_high(l, 2 + m, m, yg[:, m, :])
                for hh in range(HEADS):
                    act.wait_ge(S["head_o"], HEADS * l + hh + 1)
                    fn(hsq[:, hh, :], bank[hh][:], ACT.Square).then_inc(S["head_sq"], 1)
                for hh in range(HEADS):
                    act.wait_ge(S["head_ssq"], HEADS * l + hh + 1)
                    i = fn(hrs[:, hh, :], bank[4 + hh], ACT.Ln, bias=eps, scale=1.0 / P)
                link(i)
                for hh in range(HEADS):
                    fn(hrs[:, hh, :], hrs[:, hh, :], ACT.Exp, scale=-0.5).then_inc(S["head_rstd"], 1)
                for hh in range(HEADS):
                    mix_high(l, 4 + hh, 4 + hh, q[:, hh, :])
                for m in range(DK):
                    act.wait_ge(S["used"], units_before(l) + PROJ + m + 1)
                    mixer_high(l, PROJ + m + NH)

            def ffn_group(l, n, W, ahead=NH):
                for i in range(GU):
                    act.wait_ge(S["used"], group_unit(l, n, i))
                    if i < 2 * GJ and i % 2 == 0:
                        j = i // 2
                        act.wait_ge(S["g_t"], GJ * n + j + 1)
                        fn(sil[:, j % 2, 0:W], bank[2 * (j % 2)][:, 0:W], ACT.Silu).then_inc(S["silu"], 1)
                    if i < GU - NH or ahead:
                        group_high(l, n, i + NH)
                    if i < 2 * GJ and i % 2 == 1:
                        j = i // 2
                        act.wait_ge(S["g_t"], GJ * n + j + 3)
                        fn(gh[:, j, 0:W], gt[:, j % 2, 0:W], ACT.Copy).then_inc(S["g_hi"], 1)

            def norm_of_h(n, split=True):
                norm_rstd("sums", n + 1, sum_bank(n), rstd, D, "rstd_ready")
                if split:
                    for kk in range(DK):
                        act.wait_ge(S["xt"], DK * n + kk + 1)
                        fn(xh[:, kk, :], xt[:, kk % 4, :], ACT.Copy).then_inc(S["xt_hi"], 1)

            def gather(e, W):
                for m in range(DK):
                    act.wait_ge(S["gather"], DK * e + m + 1)
                    fn(xe[:, m, 0:W], bank[m % 4][:, 0:W], ACT.Copy).then_inc(S["gather_evac"], 1)
                act.wait_ge(S["gates"], e + 1)
                fn(gslot[:, 0, 0:W // P], bank[0][:, 0:W // P], ACT.Copy).then_inc(S["gates_evac"], 1)

            def groups(e, W):
                with act.Fori(0, NG) as gi:
                    n = e * NG + gi + NG
                    for j in range(GJ):
                        act.wait_ge(S["used"], group_unit(1, n, 2 * j))
                        act.wait_ge(S["g_cnt"], GJ * n + j - 1)
                        fn(sil[:, j % 2, 0:W], bank[2 * (j % 2)][:, 0:W], ACT.Silu).then_inc(S["silu"], 1)
                act.wait_ge(S["gates_evac"], e + 1)
                fn(gslot[:, 1, 0:W // P], gslot[:, 0, 0:W // P], ACT.Copy).then_inc(S["gates_kept"], 1)

            def tail(e, tiles):
                act.wait_ge(S["gates_kept"], e + 1)
                for n in range(2 * tiles):
                    act.wait_ge(S["yT"], 8 * e + n + 1)
                    fn(yh[:, n // 2, (n % 2) * T:(n % 2 + 1) * T], bank[4 + n % 4], ACT.Copy,
                       scale=gslot[:, 1, n // 2:n // 2 + 1]
                       ).then_inc(S["yT_hi"], 1 if n + 1 < 2 * tiles else 9 - 2 * tiles)

            def count_of(e):
                return act.value_load(cnt_i[0:1, bass.ds(e, 1)], min_val=-1, max_val=T)

            def by_half(n, body):
                with act.If(n <= NARROW):
                    body(NARROW)
                with act.Else():
                    body(T)

            def by_tiles(n, body):
                with act.If(n <= P):
                    body(1)
                with act.Else():
                    with act.If(n <= 2 * P):
                        body(2)
                    with act.Else():
                        body(4)
                    act.nop()

            for l in range(DEPTH):
                for u in range(NH):
                    mixer_high(l, u)
                if l == 0:
                    act.wait_ge(S["const_in"], 16)
                norm_of_h(2 * l)
                mixers(l)
                if l == 0:
                    act.wait_ge(S["used"], units_before(l) + MIX)
                    for i in range(NH):
                        group_high(l, NG * l, i)
                norm_of_h(2 * l + 1, split=(l == 0))
                if l == 0:
                    with act.Fori(0, NG - 1) as gi:
                        ffn_group(0, gi, T)
                    ffn_group(0, NG - 1, T, ahead=0)
            for n in range(8):
                act.wait_ge(S["xtok"], n + 1)
                fn(xtok[:, n // 2, (n % 2) * T:(n % 2 + 1) * T], bank[4 + n % 4], ACT.Copy
                   ).then_inc(S["xtok_evac"], 1)
            act.wait_ge(S["route_exp"], 1)
            fn(w2nd, dlt, ACT.Exp).then_inc(S["route_exp"], 1)
            act.wait_ge(S["counts_ready"], 1)
            for e in range(E):
                act.wait_ge(S["bc"], e + 1)
                fn(place[:, e, :], bank[4 + e % 2], ACT.Copy).then_inc(S["bc_evac"], 1)
            by_half(count_of(0), lambda W: gather(0, W))
            with act.Fori(0, E) as e:
                n_tok = count_of(e)
                by_half(n_tok, lambda W: groups(e, W))
                n_next = count_of(e + 1)
                by_tiles(n_tok, lambda tiles: tail(e, tiles))
                with act.If(n_next >= 0):
                    by_half(n_next, lambda W: gather(e + 1, W))
                    act.nop()
                with act.Else():
                    act.nop().then_inc(S["gates_evac"], 1)
            norm_of_h(2 * DEPTH, split=False)

        @block.vector
        def _(dve):
            V = nc.vector
            link = chain(dve, S["dve"])
            tt, ts, stt = V.tensor_tensor, V.tensor_scalar, V.scalar_tensor_tensor
            MUL, ADD, SUB = ALU.mult, ALU.add, ALU.subtract

            def square(kk):
                tt(sq[:, kk, :], h[:, kk, :], h[:, kk, :], MUL).then_inc(S["squares"], 1)

            def norm_of_h(n, gain, dst, done):
                dve.wait_ge(S["rstd_ready"], n + 1)
                for kk in range(DK + 1):
                    if kk < DK and dst is not None:
                        stt(dst[:, kk, :], h[:, kk, :], gain[:, kk:kk + 1], rstd, MUL, MUL).then_inc(S[done], 1)
                    elif kk < DK:
                        if kk >= 4:
                            dve.wait_ge(S["xn_odd" if kk % 2 else "xn_ready"], 4 * n + (kk - 4) // 2 + 1)
                        stt(xt[:, kk % 4, :], h[:, kk, :], gain[:, kk:kk + 1], rstd, MUL, MUL).then_inc(S["xt"], 1)
                    if dst is None and kk >= 2 and kk % 2 == 0:
                        m = kk - 2
                        dve.wait_ge(S["xt_hi"], DK * n + m + 1)
                        tt(xl[:, m, :], xt[:, m % 4, :], xh[:, m, :].bitcast(F32), SUB).then_inc(S["xn_ready"], 1)

            def s5_discretise(l):
                sm = lambda i: small[:, i, :]
                V.memset(R3, 0.0).then_inc(S["s5_zero"], 1)
                dve.wait_ge(S["s5_dt"], l + 1)
                tt(sm(1), PR(l, "lam_re"), sm(0), MUL)
                link(tt(sm(2), PR(l, "lam_im"), sm(0), MUL))
                import math
                magic = 1.5 * 2.0 ** 23
                link(ts(sm(8), sm(2), 1.0 / (2 * math.pi), magic, MUL, ADD))
                link(ts(sm(8), sm(8), magic, None, SUB))
                for part in (6.28125, 0.0019350051879882812, 3.0199159819e-07):
                    link(stt(sm(2), sm(8), -part, sm(2), MUL, ADD))
                link(ts(sm(4), sm(2), math.pi * (1 - 1e-7), -math.pi * (1 - 1e-7), ALU.min, ALU.max))
                link(ts(sm(6), sm(4), -1.0, None, MUL))
                link(tt(sm(6), sm(6), sm(4), ALU.max))
                ts(sm(6), sm(6), -1.0, math.pi / 2, MUL, ADD).then_inc(S["s5_args"], 1)
                dve.wait_ge(S["s5_sin"], l + 1)
                pr_, pi_ = pw[:, 0], pw[:, 1]
                link(V.memset(pr_[:, :, 0], 1.0))
                link(V.memset(pi_[:, :, 0], 0.0))
                link(tt(pr_[:, :, 1], sm(3), sm(7), MUL))
                link(tt(pi_[:, :, 1], sm(3), sm(5), MUL))

                def powers(a, n, by):
                    src = lambda r: pw[:, r, :, a:a + n]
                    mul = lambda r: pw[:, r, :, by:by + 1].to_broadcast([P, PAIRS, n])
                    dst = lambda r: pw[:, r, :, a + by:a + by + n]
                    tmp = lambda i: small[:, 16 + 4 * i:20 + 4 * i, :].rearrange("p a q -> p (a q)")[
                        :, 0:PAIRS * n].rearrange("p (q n) -> p q n", n=n)
                    tt(tmp(0), src(0), mul(0), MUL)
                    tt(tmp(1), src(1), mul(1), MUL)
                    tt(tmp(2), src(0), mul(1), MUL)
                    link(tt(tmp(3), src(1), mul(0), MUL))
                    tt(dst(0), tmp(0), tmp(1), SUB)
                    link(tt(dst(1), tmp(2), tmp(3), ADD))
                powers(1, 1, 1)
                powers(1, 2, 2)
                powers(1, 4, 4)
                link(ts(sm(9), pr_[:, :, 1], 1.0, None, SUB))
                lr, li_ = PR(l, "lam_re"), PR(l, "lam_im")
                tt(sm(10), lr, lr, MUL)
                link(tt(sm(11), li_, li_, MUL))
                link(tt(sm(10), sm(10), sm(11), ADD))
                link(V.reciprocal(sm(10), sm(10)))
                tt(sm(11), sm(9), lr, MUL)
                tt(sm(12), pi_[:, :, 1], li_, MUL)
                tt(sm(13), pi_[:, :, 1], lr, MUL)
                link(tt(sm(14), sm(9), li_, MUL))
                tt(sm(11), sm(11), sm(12), ADD)
                link(tt(sm(13), sm(13), sm(14), SUB))
                tt(sm(11), sm(11), sm(10), MUL)
                link(tt(sm(13), sm(13), sm(10), MUL))
                v3 = lambda n: PR(l, n).rearrange("p (q c) -> p q c", q=PAIRS)
                br, bi, cr, ci = v3("b_re"), v3("b_im"), v3("c_re"), v3("c_im")
                bc = lambda a: a.unsqueeze(2).to_broadcast([P, PAIRS, S5_C])
                tq = [Wtmp[:, i * P:(i + 1) * P].rearrange("p (q c) -> p q c", q=PAIRS) for i in range(4)]
                tt(tq[0], br, bc(sm(11)), MUL)
                tt(tq[1], bi, bc(sm(13)), MUL)
                tt(tq[2], br, bc(sm(13)), MUL)
                link(tt(tq[3], bi, bc(sm(11)), MUL))
                tt(bb[:, 0], tq[0], tq[1], SUB)
                link(tt(bb[:, 1], tq[2], tq[3], ADD))
                n = S5_T
                shape = [P, PAIRS, n, S5_C]
                pb = lambda r, n: pw[:, r, :, 0:n].unsqueeze(3).to_broadcast([P, PAIRS, n, S5_C])
                b4 = lambda a, n: a.unsqueeze(2).to_broadcast([P, PAIRS, n, S5_C])
                w4 = lambda n: Wtmp[:, 0:PAIRS * n * S5_C].rearrange("p (q s c) -> p q s c", q=PAIRS, s=n)
                link(tt(Wst[:, :, 0], pb(0, n), b4(bb[:, 0], n), MUL))
                link(tt(w4(n), pb(1, n), b4(bb[:, 1], n), MUL))
                link(tt(Wst[:, :, 0], Wst[:, :, 0], w4(n), SUB))
                link(tt(Wst[:, :, 1], pb(0, n), b4(bb[:, 1], n), MUL))
                link(tt(w4(n), pb(1, n), b4(bb[:, 0], n), MUL))
                tt(Wst[:, :, 1], Wst[:, :, 1], w4(n), ADD).then_inc(S["s5_w"], 1)
                dve.wait_ge(S["s5_w"], l + 1)
                n = S5_T + 1
                link(tt(cp[0], pb(0, n), b4(cr, n), MUL))
                link(tt(w4(n), pb(1, n), b4(ci, n), MUL))
                link(tt(cp[0], cp[0], w4(n), SUB))
                link(tt(cp[1], pb(1, n), b4(cr, n), MUL))
                link(tt(w4(n), pb(0, n), b4(ci, n), MUL))
                stt(cp[1], cp[1], -1.0, w4(n), MUL, SUB).then_inc(S["s5_bc"], 1)

            def hgrn_bounds_in(l):
                a0, a1 = PR(0, "lb0"), PR(0, "lb1")
                link(tt(omx[:, 16:20], a0, a1, ALU.max))
                tt(omx[:, 0:4], a0, omx[:, 16:20], SUB)
                tt(omx[:, 4:8], a1, omx[:, 16:20], SUB).then_inc(S["lb_in"], 1)

            def hgrn_bounds(l):
                dve.wait_ge(S["lb_exp"], l + 1)
                link(tt(omx[:, 20:24], omx[:, 8:12], omx[:, 12:16], ADD))
                link(V.reciprocal(omx[:, 20:24], omx[:, 20:24]))
                tt(omx[:, 24:28], omx[:, 8:12], omx[:, 20:24], MUL)
                link(tt(omx[:, 28:32], omx[:, 12:16], omx[:, 20:24], MUL))
                if l == 0:
                    link(tt(lbm, omx[:, 24:28], omx[:, 24:28], SUB))
                else:
                    link(tt(lbm, omx[:, 24:28], omx[:, 28:32], ADD))
                    link(tt(lbm, lbm, omx[:, 24:28], SUB))
                link(ts(lbm, lbm, 0.0, 1.0 - 1e-6, ALU.max, ALU.min))
                link(ts(oml, lbm, -1.0, 1.0, MUL, ADD))
                link(ts(lbm, lbm, 1e-30, None, ALU.max))

            def conv(l):
                w = PR(l, "conv_w")
                dve.wait_ge(S["proj_evac"], PROJ * l + 8)
                for m in range(2):
                    gb, z, vv = ucv[:, 2 + m, :], ucv[:, 4 + m, :], ucv[:, 6 + m, :]
                    link(tt(z, z, vv, MUL))
                    col = lambda tap: w[:, 2 * tap + m:2 * tap + m + 1]
                    link(ts(vv, z, col(2), None, MUL))
                    link(stt(vv[:, 1:T], z[:, 0:T - 1], col(1), vv[:, 1:T], MUL, ADD))
                    link(stt(vv[:, 2:T], z[:, 0:T - 2], col(0), vv[:, 2:T], MUL, ADD))
                    link(tt(vv, vv, gb, MUL))
                    i = tt(z, vv, vv, MUL)
                    if m == 0:
                        link(i)
                    else:
                        i.then_inc(S["conv_sq_in"], 1)

            def s5_rows(l):
                dve.wait_ge(S["proj_evac"], PROJ * l + 2)
                dve.wait_ge(S["s5_wT"], 4 * (l + 1))
                for j in range(2):
                    i = V.tensor_copy(us[:, j], ucv[:, j, :].rearrange("p (n s) -> p s n", s=S5_T))
                    if j == 0:
                        link(i)
                i.then_inc(S["s5_us"], 1)

            def s5_scan(l):
                dve.wait_ge(S["s5_v"], l + 1)
                dve.wait_ge(S["s5_T_in"], 16 * S5_T * (l + 1))
                for r in range(2):
                    i = V.tensor_copy(X[:, r].rearrange("p q n -> p (q n)"), bank[4 + r])
                link(i)
                a = lambda i: small[:, 32 + i, :]
                V.tensor_copy(a(0), pw[:, 0, :, S5_T])
                link(V.tensor_copy(a(1), pw[:, 1, :, S5_T]))
                d = 1
                while d < S5_NC:
                    n = S5_NC - d
                    for r in range(2):
                        src = X[:, r, :, 0:n]
                        tt(t1[:, r, :, 0:n], src, a(0).unsqueeze(2).to_broadcast([P, PAIRS, n]), MUL)
                        i = tt(t2[:, r, :, 0:n], src, a(1).unsqueeze(2).to_broadcast([P, PAIRS, n]), MUL)
                    link(i)
                    for r in range(2):
                        i = tt(X[:, r, :, d:], X[:, r, :, d:], t1[:, r, :, 0:n], ADD)
                    link(i)
                    tt(X[:, 0, :, d:], X[:, 0, :, d:], t2[:, 1, :, 0:n], SUB)
                    i = tt(X[:, 1, :, d:], X[:, 1, :, d:], t2[:, 0, :, 0:n], ADD)
                    d *= 2
                    if d < S5_NC:
                        link(i)
                        tt(a(2), a(0), a(0), MUL)
                        tt(a(3), a(1), a(1), MUL)
                        link(tt(a(4), a(0), a(1), MUL))
                        tt(a(0), a(2), a(3), SUB)
                        link(ts(a(1), a(4), 2.0, None, MUL))
                    else:
                        i.then_inc(S["s5_x"], 1)
                    if d == 8:
                        decays_in(l)

            def mix_low(l, n, tile, src):
                dve.wait_ge(S["mix_h"], DK * l + n + 1)
                tt(xl[:, tile, :], src, xh[:, tile, :].bitcast(F32), SUB).then_inc(S["mix_ready"], 1)

            def conv_gain(l):
                dve.wait_ge(S["conv_rstd"], l + 1)
                for m in range(2):
                    y = ucv[:, 6 + m, :]
                    link(stt(y, y, PR(l, "conv_norm")[:, m:m + 1], s5_rstd, MUL, MUL))

            def s5_yd(l):
                dve.wait_ge(S["s5_y_in"], 16 * (l + 1))
                for j in range(2):
                    i = stt(yg[:, j, :].rearrange("p (n s) -> p n s", s=S5_T),
                            ucv[:, j, :].rearrange("p (n s) -> p n s", s=S5_T), PR(l, "s5_d")[:, j:j + 1],
                            ych[:, j].rearrange("p s n -> p n s"), MUL, ADD)
                i.then_inc(S["s5_yd"], 1)

            def s5_gated(l):
                dve.wait_ge(S["s5_sig"], l + 1)
                link(tt(yg, yg, ysg, MUL))
                tt(sq2, yg, yg, MUL).then_inc(S["s5_sq"], 1)

            def s5_gain(l):
                dve.wait_ge(S["s5_rstd"], l + 1)
                for m in range(2):
                    link(stt(yg[:, m, :], yg[:, m, :], PR(l, "s5_norm")[:, m:m + 1], s5_rstd, MUL, MUL))
                V.nop().then_inc(S["mix_t"], 2)

            def s5_mix(l):
                for n, (tile, src) in enumerate([(2, ucv[:, 6, :]), (3, ucv[:, 7, :]), (0, yg[:, 0, :]),
                                                 (1, yg[:, 1, :])]):
                    mix_low(l, n, tile, src)
                dve.wait_ge(S["mix_ready"], 4 * (l + 1))
                V.nop().then_inc(S["s5_mix"], 1)

            def halves(a, m, which):
                return a.rearrange("p (b w m) -> p b w m", w=2, m=m)[:, :, which, :]

            def decays_in(l):
                TINY = 2.0 ** -60
                dve.wait_ge(S["proj_evac"], PROJ * l + 12)
                for hh in range(HEADS):
                    ts(f[:, hh, :], f[:, hh, :], oml[:, hh:hh + 1], lbm[:, hh:hh + 1], MUL, ADD)
                    i = ts(k[:, hh, :], k[:, hh, :], oml[:, hh:hh + 1], None, MUL)
                link(i)
                dve.wait_ge(S["s5_v"], l + 1)
                link(ts(ftail, f, 1.0 / TINY, 1.0, MUL, ALU.min))
                ts(f, f, TINY, None, ALU.max).then_inc(S["f_in"], 1)

            def decays_sum(l):
                dve.wait_ge(S["f_ln"], l + 1)
                link(tt(ftail, ftail, f, ADD))
                for hh in range(HEADS):
                    for c in range(NCH):
                        cols = slice(c * CH, (c + 1) * CH)
                        i = V.tensor_tensor_scan(f[:, hh, cols], ones, ftail[:, hh, cols], 0.0, MUL, ADD)
                i.then_inc(S["b_ready"], 1)
                dve.wait_ge(S["b_ready"], l + 1)

            def hgrn(l):
                dve.wait_ge(S["s5_y"], 2 * (l + 1))
                fb, fk, fq = (a.rearrange("p h t -> p (h t)") for a in (f, k, q))
                n_lv = len(LEVELS)

                def diff(li):
                    m = LEVELS[li]
                    e = EB[li % 2]
                    if li >= 2:
                        dve.wait_ge(S["score"], N_SC * l + HEADS * li)
                    ref = halves(fb, m, 0)[:, :, m - 1:m].to_broadcast([P, 2048 // (2 * m), m])
                    tt(halves(e, m, 0), ref, halves(fb, m, 0), SUB)
                    tt(halves(e, m, 1), halves(fb, m, 1), ref, SUB).then_inc(S["b_diff"], 1)

                def use_scores(s):
                    if s > 0:
                        dve.wait_ge(S["score_used"], N_SC * l + HEADS * s)
                    for hh in range(HEADS):
                        dve.wait_ge(S["score"], N_SC * l + HEADS * s + hh + 1)
                        V.copy_predicated(PT[:, hh, :].rearrange("p (c t) -> p c t", c=NCH),
                                          msk[:, (s - 1) % (n_lv + 1), :].unsqueeze(1).to_broadcast([P, NCH, P]),
                                          bank[hh + 4][:].rearrange("p (c t) -> p c t", c=NCH)
                                          ).then_inc(S["score_used"], 1)

                diff(0)
                link(V.memset(R3, 0.0))
                dve.wait_ge(S["proj_evac"], PROJ * l + 16)
                for li in range(n_lv):
                    m = LEVELS[li]
                    if li + 1 < n_lv:
                        diff(li + 1)
                    dve.wait_ge(S["b_exp"], n_lv * l + li + 1)
                    e = EB[li % 2]
                    tt(halves(e, m, 0), halves(e, m, 0), halves(fk, m, 0), MUL)
                    tt(halves(e, m, 1), halves(e, m, 1), halves(fq, m, 1), MUL).then_inc(S["b_mul"], 1)
                    use_scores(li)
                    if li == 3:
                        s5_yd(l)
                b4 = f.rearrange("p h (c t) -> p (h c) t", c=NCH)
                last = b4[:, :, CH - 1:CH].to_broadcast([P, HEADS * NCH, CH])
                tt(EB[1].rearrange("p (b t) -> p b t", t=CH), last, b4, SUB).then_inc(S["tail_diff"], 1)
                dve.wait_ge(S["tail_exp"], 2 * l + 1)
                tt(EB[1], EB[1], fk, MUL).then_inc(S["tail_mul"], 1)
                use_scores(n_lv)
                dve.wait_ge(S["tail_exp"], 2 * l + 2)
                tt(EB[0], EB[0], fq, MUL).then_inc(S["tail_mul"], 1)
                s5_gated(l)
                dve.wait_ge(S["proj_evac"], PROJ * (l + 1))
                V.nop().then_inc(S["mix_t"], 2)
                for c in range(NCH - 1):
                    dve.wait_ge(S["kv"], (NCH - 1) * l + c + 1)
                    if c == 0:
                        V.tensor_copy(St[:, 0, :], bank[4]).then_inc(S["states"], 1)
                        continue
                    dve.wait_ge(S["states"], 3 * l + c)
                    link(tt(St[:, c, :].rearrange("p (h d) -> p h d", h=HEADS),
                            St[:, c - 1, :].rearrange("p (h d) -> p h d", h=HEADS),
                            dec[:, :, c:c + 1].to_broadcast([P, HEADS, P]), MUL))
                    tt(St[:, c, :], St[:, c, :], bank[4 + c], ADD).then_inc(S["states"], 1)
                s5_gain(l)
                s5_mix(l)
                for hh in range(HEADS):
                    dve.wait_ge(S["head_rstd"], HEADS * l + hh + 1)
                    link(tt(htmp[:, hh, :], bank[hh][:], hrs[:, hh, :], MUL))
                    stt(q[:, hh, :], htmp[:, hh, :], PR(l, "hg_norm")[:, hh:hh + 1], gate[:, hh, :], MUL, MUL
                        ).then_inc(S["mix_t"], 1)

            def add_out(l):
                for m in range(DK):
                    dve.wait_ge(S["used"], units_before(l) + PROJ + m + 1)
                    tt(h[:, m, :], h[:, m, :], bank[4 + m % 2], ADD).then_inc(S["y_added"], 1)
                    dve.wait_ge(S["y_added"], DK * l + m + 1)
                    square(m)

            def low(l, n, i):
                if i >= GU:
                    n, i = n + 1, i - GU
                if i in DVE_UNITS:
                    dve.wait_ge(S["hi"], group_unit(l, n, i))
                    tt(wl[:, i % NH, :], raw(i), wh[:, i % NH, :].bitcast(F32), SUB).then_inc(S["lo_dve"], 1)

            def add_y(n, q_, acc, W, e=None):
                dve.wait_ge(S["y_cnt"], 4 * n + 2)
                if e is not None and q_ == 0:
                    dve.wait_ge(S["ye_zero"], e + 1)
                a = acc[:, 2 * q_:2 * q_ + 2, 0:W]
                tt(a, a, ybank[q_ % 2][:, :, 0:W], ADD).then_inc(S["y_cnt"], 1)

            def ffn_group(l, n, W, acc, ahead=NH):
                for i in range(GU):
                    j = i // 2
                    if i < 2 * GJ and i % 2 == 1:
                        dve.wait_ge(S["silu"], GJ * n + j + 1)
                        dve.wait_ge(S["used"], group_unit(l, n, i))
                        if j >= 2:
                            dve.wait_ge(S["g_cnt"], GJ * n + j - 1)
                        tt(gt[:, j % 2, 0:W], sil[:, j % 2, 0:W], bank[2 * (j % 2) + 1][:, 0:W], MUL
                           ).then_inc(S["g_t"], 1)
                    if i >= 2 * GJ:
                        q_ = i - 2 * GJ
                        dve.wait_ge(S["used"], group_unit(l, n, i))
                        add_y(n, q_, acc, W)
                    if i < GU - NH or ahead:
                        low(l, n, i + NH)
                    if i >= 2 * GJ and not ahead:
                        dve.wait_ge(S["y_cnt"], 4 * n + q_ + 3)
                        for m in (2 * q_, 2 * q_ + 1):
                            square(m)
                    if i < 2 * GJ and i % 2 == 1:
                        dve.wait_ge(S["g_hi"], GJ * n + j + 1)
                        tt(gl[:, j, 0:W], gt[:, j % 2, 0:W], gh[:, j, 0:W].bitcast(F32), SUB).then_inc(S["g_cnt"], 1)

            def route():
                dve.wait_ge(S["logits"], 1)
                link(V.tensor_copy(lg.rearrange("p i e -> p (i e)"), bank[0][:, 0:4 * E]))
                for i4 in range(4):
                    mine = lg[:, i4, :].unsqueeze(2).to_broadcast([P, E, E])
                    other = lg[:, i4, :].unsqueeze(1).to_broadcast([P, E, E])
                    tt(cmp3[:, i4], other, mine, ALU.is_gt)
                    link(tt(eq3[:, i4], other, mine, ALU.is_equal))
                tri = C("tri8").rearrange("p (e f) -> p e f", e=E)
                for i4 in range(4):
                    i = tt(eq3[:, i4], eq3[:, i4], tri, MUL)
                link(i)
                link(tt(cmp3, cmp3, eq3, ADD))
                link(V.tensor_reduce(rank.rearrange("p i e -> p (i e)"), cmp3.rearrange("p i e f -> p (i e) f"),
                                     AX_X, ADD))
                ts(first, rank, 0.5, None, ALU.is_lt)
                link(ts(selm, rank, 1.5, None, ALU.is_lt))
                link(tt(second, selm, first, SUB))
                V.nop().then_inc(S["route_d"], 1)
                link(tt(rtmp, lg, first, MUL))
                link(V.tensor_reduce(top1, rtmp, AX_X, ADD))
                link(tt(rtmp, lg, second, MUL))
                link(V.tensor_reduce(top2, rtmp, AX_X, ADD))
                tt(dlt, top2, top1, SUB).then_inc(S["route_exp"], 1)
                dve.wait_ge(S["route_exp"], 2)
                link(ts(w1st, w2nd, 1.0, None, ADD))
                link(V.reciprocal(w1st, w1st))
                link(tt(w2nd, w2nd, w1st, MUL))
                bc = lambda a: a.unsqueeze(2).to_broadcast([P, 4, E])
                link(tt(gatem, first, bc(w1st), MUL))
                link(tt(rtmp, second, bc(w2nd), MUL))
                link(tt(gatem, gatem, rtmp, ADD))
                dve.wait_ge(S["posT"], 1)
                link(ts(rtmp.rearrange("p i e -> p (i e)"), bank[1][:, 0:4 * E], 1.0, None, ADD))
                link(tt(rtmp, rtmp, selm, MUL))
                link(ts(posm, rtmp, 1.0, None, SUB))
                V.memset(cnt_i[:, E:E + 1], -1.0)
                link(V.tensor_copy(cnt_i[:, 0:E], bank[1][:, 4 * E:5 * E]))
                V.nop().then_inc(S["counts_ready"], 1)

            def places(e):
                if e >= 2:
                    dve.wait_ge(S["bc"], e - 1)
                for i4 in range(4):
                    i = ts(posg[:, e % 2, i4 * P:(i4 + 1) * P], ones, posm[:, i4, e:e + 1], None, MUL)
                i.then_inc(S["sel_pos"], 1)

            def one_hot_tokens(e):
                for i4 in range(4):
                    i = ts(sel[:, i4, :], C("iota"), pos9[:, i4, bass.ds(e, 1)], None, ALU.is_equal)
                i.then_inc(S["sel_ready"], 1)

            V.nop().then_inc(S["g_t"], 2)
            V.nop().then_inc(S["y_cnt"], 2)
            V.nop().then_inc(S["scatter_added"], DK // 2)
            V.nop().then_inc(S["lo_dve"], ND_)

            def groups(e, W):
                for s in range(W // P):
                    i = ts(G[:, s, :], place[:, bass.ds(e, 1), :].rearrange("p a t -> p (a t)"), C("slot")[:, s:s + 1],
                           None, ALU.is_equal)
                i.then_inc(S["G_ready"], 1)
                V.memset(ye[:, :, 0:W], 0.0).then_inc(S["ye_zero"], 1)
                with dve.Fori(0, NG) as gi:
                    n = e * NG + gi + NG
                    for j in range(GJ):
                        dve.wait_ge(S["silu"], GJ * n + j + 1)
                        dve.wait_ge(S["used"], group_unit(1, n, 2 * j + 1))
                        tt(g[:, j, 0:W], sil[:, j % 2, 0:W], bank[2 * (j % 2) + 1][:, 0:W], MUL
                           ).then_inc(S["g_cnt"], 1)
                    for q_ in range(4):
                        dve.wait_ge(S["used"], group_unit(1, n, 2 * GJ + q_))
                        add_y(n, q_, ye, W, e)

            def tail(e, tiles):
                for n in range(2 * tiles):
                    dve.wait_ge(S["yT_hi"], 8 * e + n + 1)
                    stt(yl[:, n // 2, (n % 2) * T:(n % 2 + 1) * T], bank[4 + n % 4], gslot[:, 1, n // 2:n // 2 + 1],
                        yh[:, n // 2, (n % 2) * T:(n % 2 + 1) * T].bitcast(F32), MUL, SUB
                        ).then_inc(S["yT_lo"], 1 if n + 1 < 2 * tiles else 9 - 2 * tiles)
                for m2 in range(DK // 2):
                    dve.wait_ge(S["scatter"], DK // 2 * e + m2 + 1)
                    tt(h[:, 2 * m2:2 * m2 + 2, :], h[:, 2 * m2:2 * m2 + 2, :], pair[m2][:], ADD
                       ).then_inc(S["scatter_added"], 1)

            def count_of(e):
                return dve.value_load(cnt_i[0:1, bass.ds(e, 1)], min_val=-1, max_val=T)

            for l in range(DEPTH):
                if l == 0:
                    for kk in range(DK):
                        dve.wait_ge(S["x_in" if kk < DK // 2 else "x_in_late"], 16 * DK // 2)
                        square(kk)
                    dve.wait_ge(S["par_in"], 16)
                    dve.wait_ge(S["const_in"], 16)
                norm_of_h(2 * l, PR(l, "attn_norm"), None, "xn_ready")
                hgrn_bounds_in(l)
                s5_discretise(l)
                hgrn_bounds(l)
                s5_rows(l)
                conv(l)
                if l == 0:
                    dve.wait_ge(S["glu_in"], 48)
                    link(V.tensor_copy(msk[:], R5[:, 0:(len(LEVELS) + 1) * P].rearrange("p (l t) -> p l t", t=P)))
                s5_scan(l)
                decays_sum(l)
                conv_gain(l)
                hgrn(l)
                add_out(l)
                if l == 0:
                    for i in range(NH):
                        low(l, NG * l, i)
                norm_of_h(2 * l + 1, PR(l, "ffn_norm"), xe if l else None, "xn_ready")
                if l == 0:
                    with dve.Fori(0, NG - 1) as gi:
                        ffn_group(0, gi, T, h)
                    ffn_group(0, NG - 1, T, h, ahead=0)
                    dve.wait_ge(S["y_cnt"], 4 * NG + 2)
                else:
                    route()
                    for e in range(E):
                        places(e)
                    one_hot_tokens(0)
                    dve.wait_ge(S["bc_evac"], E)
                    with dve.Fori(0, E) as e:
                        n_tok = count_of(e)
                        dve.wait_ge(S["gates"], e + 1)
                        n_next = count_of(e + 1)
                        with dve.If(n_next >= 0):
                            one_hot_tokens(e + 1)
                        with dve.If(n_tok <= NARROW):
                            groups(e, NARROW)
                        with dve.Else():
                            groups(e, T)
                        with dve.If(n_tok <= P):
                            tail(e, 1)
                        with dve.Else():
                            with dve.If(n_tok <= 2 * P):
                                tail(e, 2)
                            with dve.Else():
                                tail(e, 4)
                            dve.nop()
                        dve.wait_ge(S["scatter_added"], DK // 2 * (e + 2))
            for kk in range(DK):
                square(kk)
            norm_of_h(2 * DEPTH, PR(0, "final_norm"), sq, "out_ready")


def _layouts(i):
    import numpy as np
    f = np.float32
    o = {}
    o["x"] = i["x"][0].T.reshape(DK, P, T)
    order = list(range(0, 8)) + list(range(12, 16)) + list(range(8, 12)) + list(range(16, 24))
    w = i["w_in"].reshape(DEPTH, DK, P, PROJ, P)[:, :, :, order, :].transpose(0, 3, 2, 1, 4)
    w_o = i["w_out"].reshape(DEPTH, DK, P, DK, P).transpose(0, 3, 2, 1, 4)
    o["wmix"] = np.concatenate([w, w_o], 1).reshape(DEPTH, MIX, P, UW)

    def ffn(w1, w3, w2):
        n = w1.shape[0]
        a = np.empty((n, NG, GU, P, UW), f)
        for w, src in enumerate((w1, w3)):
            a[:, :, w:2 * GJ:2] = src.reshape(n, DK, P, NG, GJ, P).transpose(0, 3, 4, 2, 1, 5).reshape(n, NG, GJ, P, UW)
        a[:, :, 2 * GJ:] = w2.reshape(n, NG, GJ, P, 4, 2, P).transpose(0, 1, 4, 3, 5, 2, 6).reshape(n, NG, 4, P, UW)
        return a.reshape(n * NG, GU, P, UW)
    o["wa"] = ffn(i["ffn_w1"], i["ffn_w3"], i["ffn_w2"])
    o["we"] = ffn(i["moe_w1"][0], i["moe_w3"][0], i["moe_w2"][0])

    def tiles(a):
        return a.reshape(-1, P).T

    def states(a):
        a = a.reshape((PAIRS, 2 * S5_N) + a.shape[2:])
        return np.moveaxis(a, 0, 1).reshape(P, -1)
    rows = []
    for l in range(DEPTH):
        c = lambda a: states(a.transpose(0, 2, 1))
        parts = dict(
            attn_norm=tiles(i["attn_norm"][l]), ffn_norm=tiles(i["ffn_norm"][l]), final_norm=tiles(i["final_norm"]),
            lam_re=states(i["s5_lambda_re"][l]), lam_im=states(i["s5_lambda_im"][l]),
            log_dt=states(np.broadcast_to(i["s5_log_dt"][l][:, None], (S5_G, S5_N))),
            b_re=states(i["s5_b_re"][l]), b_im=states(i["s5_b_im"][l]),
            c_re=c(i["s5_c_re"][l]), c_im=c(i["s5_c_im"][l]),
            s5_d=tiles(i["s5_d"][l]), s5_norm=tiles(i["s5_out_norm"][l]),
            conv_w=tiles(i["conv_w"][l]), conv_norm=tiles(i["conv_out_norm"][l]), hg_norm=tiles(i["hg_out_norm"][l]),
            lb0=tiles(i["hg_lower_bounds"][0]), lb1=tiles(i["hg_lower_bounds"][1]))
        rows.append(np.concatenate([parts[n] for n, _ in PARAMS], 1))
    o["par"] = np.stack(rows, 1)
    o["glu"] = i["s5_glu"].reshape(DEPTH, 2, P, 256).transpose(2, 0, 1, 3)
    o["router"] = i["moe_router"][0].reshape(DK, P, E).transpose(1, 0, 2)
    return {k: np.ascontiguousarray(v) for k, v in o.items()}


def _constants():
    import numpy as np
    p = np.arange(P)
    t = np.arange(T)
    e = np.arange(E)
    c = dict(ones=np.ones((P, P)), ident=np.eye(P), before=(p[:, None] < p[None, :]),
             tri8=np.broadcast_to((e[None, :] < e[:, None]).reshape(1, 64), (P, 64)),
             iota=np.broadcast_to(t, (P, T)),
             slot=p[:, None] + P * np.arange(4)[None, :], eps=np.full((P, 1), EPS))
    const = np.concatenate([c[n].astype(np.float32) for n, _ in CONSTS], 1)
    s, q = p[:, None], p[None, :]
    ms = [(s // (2 * m) == q // (2 * m)) & (s % (2 * m) < m) & (q % (2 * m) >= m) for m in LEVELS] + [s == q]
    return np.ascontiguousarray(const), np.ascontiguousarray(np.stack(ms, 1).astype(np.float32))


def kernel(**inputs):
    import numpy as np
    import concourse.bacc as bacc
    from concourse import mybir as mb
    from concourse.bass_utils import run_bass_kernel_spmd

    nc = bacc.Bacc("TRN2", target_bir_lowering=False, num_devices=1)
    arrays = _layouts({k: np.asarray(v) for k, v in inputs.items()})
    arrays["const"], arrays["masks"] = _constants()
    names = ["x", "wmix", "wa", "we", "par", "glu", "router", "const", "masks"]
    args = [nc.dram_tensor("in_" + n, arrays[n].shape, mb.dt.from_np(arrays[n].dtype), kind="ExternalInput").ap()
            for n in names]
    out = nc.dram_tensor("out", (DK, P, T), mb.dt.float32, kind="ExternalOutput").ap()
    build(nc, *args, out)
    r = run_bass_kernel_spmd(nc, [{"in_" + n: arrays[n] for n in names}], core_ids=[0])
    y = r.results[0]["out"]
    return np.ascontiguousarray(y.reshape(D, T).T.reshape(1, T, D))
```
